# Optimizing a Trainium2 kernel written in Bass

```python
import math
import jax, jax.numpy as jnp
from jax import lax
import numpy as np

D_MODEL = 1024
BATCH = 1
SEQ = 512
DEPTH = 1

EPS = 1e-6
A_GROUPS = 8
A_GROUP_DIM = D_MODEL // A_GROUPS
A_WIDTH = A_GROUPS * A_GROUP_DIM
CHUNK = 128
B_HEADS = 8
B_HEAD_DIM = D_MODEL // 16
B_V_DIM = 2 * B_HEAD_DIM
QK_WIDTH = B_HEADS * 2 * B_HEAD_DIM
B_WIDTH = B_HEADS * B_V_DIM
Q_BLOCK = 128
IN_COLS = 2 * A_WIDTH + 2 * QK_WIDTH + B_WIDTH
N_GROUPS = 4
EXPERTS_PER_GROUP = 8
N_EXPERTS = N_GROUPS * EXPERTS_PER_GROUP
TOP_K = 2
D_EXPERT = D_MODEL // 4
MOE_BLOCK = 128


def rmsnorm(x, g):
    xf = x.astype(jnp.float32)
    r = lax.rsqrt(jnp.mean(xf * xf, axis=-1, keepdims=True) + EPS)
    return (xf * r).astype(x.dtype) * g

def chunked_spatial_gating(u, v, g_v, w_s, b_s):
    bsz, s, _ = u.shape
    nc = s // CHUNK
    v = rmsnorm(v.reshape(bsz, s, A_GROUPS, A_GROUP_DIM), g_v)
    v = v.reshape(bsz, nc, CHUNK, A_GROUPS, A_GROUP_DIM)
    causal = jnp.tril(jnp.ones((CHUNK, CHUNK), dtype=bool))
    ws = jnp.where(causal[None], w_s, 0.0)
    z = jnp.einsum('gts,bcsgd->bctgd', ws, v) + b_s.T[None, None, :, :, None]
    return u * z.reshape(bsz, s, A_WIDTH)

def diff_attention(q, k, v, lam, slopes):
    bsz, nh, _, s, hd = q.shape
    nb = s // Q_BLOCK
    key_pos = jnp.arange(s)
    scale = hd ** -0.5

    def block(i):
        start = i * Q_BLOCK
        qb = lax.dynamic_slice_in_dim(q, start, Q_BLOCK, axis=3)
        sc = jnp.einsum('bhcqd,bhckd->bhcqk', qb, k,
                        preferred_element_type=jnp.float32) * scale
        q_pos = start + jnp.arange(Q_BLOCK)
        dist = (q_pos[:, None] - key_pos[None, :]).astype(jnp.float32)
        alibi = -slopes[:, None, None] * jnp.abs(dist)[None]
        sc = jnp.where((dist >= 0)[None, None, None], sc + alibi[None, :, None], -jnp.inf)
        p = jax.nn.softmax(sc, axis=-1)
        a = p[:, :, 0] - lam * p[:, :, 1]
        return jnp.einsum('bhqk,bhkd->bhqd', a.astype(v.dtype), v)

    out = lax.map(block, jnp.arange(nb))
    return out.transpose(1, 2, 0, 3, 4).reshape(bsz, nh, s, v.shape[-1])

def hierarchical_moe(h, w_rg, b_rg, w_re, b_re, w1, w3, w2):
    bsz, s, d = h.shape
    t = h.reshape(-1, d)
    n_tok = t.shape[0]
    g_prob = jax.nn.softmax((t @ w_rg + b_rg).astype(jnp.float32), axis=-1)
    g_gate, g_idx = lax.top_k(g_prob, 1)
    e_logits = (t @ w_re + b_re).astype(jnp.float32).reshape(n_tok, N_GROUPS, EXPERTS_PER_GROUP)
    e_logits = jnp.take_along_axis(e_logits, g_idx[:, :, None], axis=1)[:, 0]
    e_w, e_idx = lax.top_k(jax.nn.softmax(e_logits, axis=-1), TOP_K)
    e_w = e_w / jnp.sum(e_w, axis=-1, keepdims=True)
    weight = g_gate * e_w
    expert_id = g_idx * EXPERTS_PER_GROUP + e_idx
    combine = jnp.sum(jax.nn.one_hot(expert_id, N_EXPERTS, dtype=jnp.float32)
                      * weight[..., None], axis=1)

    def expert_block(args):
        tk, c = args
        hid = jax.nn.silu(jnp.einsum('td,edf->tef', tk, w1)) * jnp.einsum('td,edf->tef', tk, w3)
        hid = hid * c[:, :, None].astype(hid.dtype)
        return jnp.einsum('tef,efd->td', hid, w2)

    y = lax.map(expert_block, (t.reshape(-1, MOE_BLOCK, d),
                               combine.reshape(-1, MOE_BLOCK, N_EXPERTS)))
    return y.reshape(bsz, s, d)

def first_inputs(seed: int = 0) -> dict:
    key = jax.random.key(seed)
    ks = jax.random.split(key, 32)
    f32 = jnp.float32
    L, D = DEPTH, D_MODEL

    def nrm(k, shape, scale):
        return jax.random.normal(k, shape, f32) * scale

    def gain(k, shape):
        return 1.0 + 0.02 * jax.random.normal(k, shape, f32)

    return {
        "x": jax.random.normal(ks[0], (BATCH, SEQ, D), f32),
        "norm1_g": gain(ks[1], (L, D)),
        "w_in": nrm(ks[2], (L, D, IN_COLS), D ** -0.5),
        "v_norm_g": gain(ks[3], (L, A_GROUPS, A_GROUP_DIM)),
        "w_s": nrm(ks[4], (L, A_GROUPS, CHUNK, CHUNK), CHUNK ** -0.5),
        "b_s": 1.0 + 0.02 * jax.random.normal(ks[5], (L, A_GROUPS, CHUNK), f32),
        "q_norm_g": gain(ks[6], (L, B_HEAD_DIM)),
        "k_norm_g": gain(ks[7], (L, B_HEAD_DIM)),
        "lambda_q1": nrm(ks[8], (L, B_HEAD_DIM), 0.1),
        "lambda_k1": nrm(ks[9], (L, B_HEAD_DIM), 0.1),
        "lambda_q2": nrm(ks[10], (L, B_HEAD_DIM), 0.1),
        "lambda_k2": nrm(ks[11], (L, B_HEAD_DIM), 0.1),
        "sub_norm_g": gain(ks[12], (L, B_V_DIM)),
        "w_up_a": nrm(ks[13], (L, A_WIDTH, D), A_WIDTH ** -0.5),
        "w_up_b": nrm(ks[14], (L, B_WIDTH, D), B_WIDTH ** -0.5),
        "w_gate": nrm(ks[15], (L, D, 2 * D), D ** -0.5),
        "b_gate": nrm(ks[16], (L, 2 * D), 0.02),
        "w_out": nrm(ks[17], (L, D, D), D ** -0.5),
        "norm2_g": gain(ks[18], (L, D)),
        "w_rg": nrm(ks[19], (L, D, N_GROUPS), D ** -0.5),
        "b_rg": nrm(ks[20], (L, N_GROUPS), 0.01),
        "w_re": nrm(ks[21], (L, D, N_EXPERTS), D ** -0.5),
        "b_re": nrm(ks[22], (L, N_EXPERTS), 0.01),
        "w1": nrm(ks[23], (L, N_EXPERTS, D, D_EXPERT), D ** -0.5),
        "w3": nrm(ks[24], (L, N_EXPERTS, D, D_EXPERT), D ** -0.5),
        "w2": nrm(ks[25], (L, N_EXPERTS, D_EXPERT, D), D_EXPERT ** -0.5),
    }

def first_block(x, norm1_g, w_in, v_norm_g, w_s, b_s, q_norm_g, k_norm_g,
              lambda_q1, lambda_k1, lambda_q2, lambda_k2, sub_norm_g,
              w_up_a, w_up_b, w_gate, b_gate, w_out, norm2_g,
              w_rg, b_rg, w_re, b_re, w1, w3, w2):
    bsz, s, d = x.shape
    slopes = jnp.exp2(-8.0 * (jnp.arange(B_HEADS) + 1) / B_HEADS)
    splits = [A_WIDTH, 2 * A_WIDTH, 2 * A_WIDTH + QK_WIDTH, 2 * A_WIDTH + 2 * QK_WIDTH]
    for l in range(DEPTH):
        lam_init = 0.8 - 0.6 * math.exp(-0.3 * l)
        h = rmsnorm(x, norm1_g[l])
        proj = h @ w_in[l]
        u, v_a, q, k, v_b = jnp.split(proj, splits, axis=-1)

        y_a = chunked_spatial_gating(u, v_a, v_norm_g[l], w_s[l], b_s[l])

        q = rmsnorm(q.reshape(bsz, s, B_HEADS, 2, B_HEAD_DIM), q_norm_g[l]).transpose(0, 2, 3, 1, 4)
        k = rmsnorm(k.reshape(bsz, s, B_HEADS, 2, B_HEAD_DIM), k_norm_g[l]).transpose(0, 2, 3, 1, 4)
        vb = v_b.reshape(bsz, s, B_HEADS, B_V_DIM).transpose(0, 2, 1, 3)
        lam = (jnp.exp(jnp.sum(lambda_q1[l].astype(jnp.float32) * lambda_k1[l].astype(jnp.float32)))
               - jnp.exp(jnp.sum(lambda_q2[l].astype(jnp.float32) * lambda_k2[l].astype(jnp.float32)))
               + lam_init)
        o = diff_attention(q, k, vb, lam, slopes)
        o = rmsnorm(o, sub_norm_g[l]) * (1.0 - lam_init)
        y_b = o.transpose(0, 2, 1, 3).reshape(bsz, s, B_WIDTH)

        gates = jax.nn.sigmoid(h @ w_gate[l] + b_gate[l])
        g_a, g_b = jnp.split(gates, 2, axis=-1)
        merged = g_a * (y_a @ w_up_a[l]) + g_b * (y_b @ w_up_b[l])
        x = x + merged @ w_out[l]

        h2 = rmsnorm(x, norm2_g[l])
        x = x + hierarchical_moe(h2, w_rg[l], b_rg[l], w_re[l], b_re[l], w1[l], w3[l], w2[l])
    return x


CHUNK_2 = 64
SB_BLOCK = 128
DN_HEADS = 4
DN_DK = 128
DN_DV = 128
DN_CONV = 4
SB_HEADS = 8
SB_DH = 64
DN_WIDTH = DN_HEADS * DN_DV
SB_WIDTH = SB_HEADS * SB_DH
N_BRANCH = 2
A_QKV1 = 2 * DN_HEADS * DN_DK + DN_WIDTH
A_Z1 = A_QKV1 + DN_WIDTH
A_B1 = A_Z1 + DN_HEADS
A_A1 = A_B1 + DN_HEADS
B_QKV1 = A_A1 + 3 * SB_WIDTH
B_Z1 = B_QKV1 + SB_WIDTH
G1 = B_Z1 + N_BRANCH * D_MODEL
PROJ_WIDTH = G1


def _rms(x, gain):
    xf = x.astype(jnp.float32)
    return xf * lax.rsqrt(jnp.mean(xf * xf, axis=-1, keepdims=True) + EPS) * gain.astype(jnp.float32)

def _l2n(x):
    return x * lax.rsqrt(jnp.sum(x * x, axis=-1, keepdims=True) + EPS)

def _causal_dwconv(u, w):
    k_len, c = w.shape
    return lax.conv_general_dilated(u, w[:, None, :].astype(u.dtype), window_strides=(1,),
                                    padding=[(k_len - 1, 0)],
                                    dimension_numbers=('NWC', 'WIO', 'NWC'),
                                    feature_group_count=c)

def _gated_delta_rule(q, k, v, g, beta):
    b, s, h, dk = q.shape
    dv = v.shape[-1]
    n = s // CHUNK_2

    def blocks(t):
        return jnp.moveaxis(t.reshape(b, n, CHUNK_2, h, -1), 3, 1)

    q = blocks(q) * dk ** -0.5
    k = blocks(k)
    v = blocks(v)
    g = jnp.moveaxis(g.reshape(b, n, CHUNK_2, h), 3, 1)
    beta = jnp.moveaxis(beta.reshape(b, n, CHUNK_2, h), 3, 1)
    gc = jnp.cumsum(g, axis=-1)
    causal = jnp.tril(jnp.ones((CHUNK_2, CHUNK_2), dtype=bool))
    strict = jnp.tril(jnp.ones((CHUNK_2, CHUNK_2), dtype=bool), -1)
    decay = jnp.exp(jnp.where(causal, gc[..., :, None] - gc[..., None, :], -jnp.inf))
    kk = jnp.einsum('bhnid,bhnjd->bhnij', k, k)
    m = jnp.where(strict, beta[..., :, None] * kk * decay, 0.0)
    eye = jnp.eye(CHUNK_2, dtype=m.dtype)
    rhs = jnp.concatenate([beta[..., None] * v,
                           beta[..., None] * k * jnp.exp(gc)[..., None]], axis=-1)
    sol = lax.linalg.triangular_solve(eye + m, rhs, left_side=True, lower=True, unit_diagonal=True)
    u, w = sol[..., :dv], sol[..., dv:]
    qk = jnp.where(causal, jnp.einsum('bhnid,bhnjd->bhnij', q, k) * decay, 0.0)
    q_dec = q * jnp.exp(gc)[..., None]
    k_dec = k * jnp.exp(gc[..., -1:] - gc)[..., None]
    g_end = jnp.exp(gc[..., -1])

    def step(state, inp):
        qk_c, qd_c, kd_c, u_c, w_c, ge_c = inp
        v_new = u_c - jnp.einsum('bhck,bhkv->bhcv', w_c, state)
        o = (jnp.einsum('bhck,bhkv->bhcv', qd_c, state)
             + jnp.einsum('bhij,bhjv->bhiv', qk_c, v_new))
        state = state * ge_c[..., None, None] + jnp.einsum('bhck,bhcv->bhkv', kd_c, v_new)
        return state, o

    xs = tuple(jnp.moveaxis(t, 2, 0) for t in (qk, q_dec, k_dec, u, w, g_end))
    state0 = jnp.zeros((b, h, dk, dv), q.dtype)
    _, o = lax.scan(step, state0, xs)
    return jnp.transpose(o, (1, 0, 3, 2, 4)).reshape(b, s, h, dv)

def _stick_breaking(q, k, v):
    _, _, s, d = q.shape
    scale = d ** -0.5
    outs = []
    for blk in range(s // SB_BLOCK):
        q0 = blk * SB_BLOCK
        end = q0 + SB_BLOCK
        z = jnp.einsum('bhqd,bhkd->bhqk', q[:, :, q0:end], k[:, :, :end]) * scale
        qi = q0 + jnp.arange(SB_BLOCK)[:, None]
        kj = jnp.arange(end)[None, :]
        mask = kj < qi
        log_keep = jnp.where(mask, jax.nn.log_sigmoid(-z), 0.0)
        rest = lax.cumsum(log_keep, axis=3, reverse=True) - log_keep
        a = jnp.where(mask, jnp.exp(jax.nn.log_sigmoid(z) + rest), 0.0)
        outs.append(jnp.einsum('bhqk,bhkd->bhqd', a, v[:, :, :end]))
    return jnp.concatenate(outs, axis=2)

def _layer(x, norm_gain, w_in, b_gate, conv_w, a_log, dt_bias, dn_out_gain,
           sb_q_gain, sb_k_gain, w_up_a, w_up_b, w_out):
    f32 = jnp.float32
    b, s, _ = x.shape
    xn = _rms(x, norm_gain).astype(x.dtype)
    proj = jnp.einsum('bsd,dp->bsp', xn, w_in)

    nqk = DN_HEADS * DN_DK
    qkv_a = jax.nn.silu(_causal_dwconv(proj[..., :A_QKV1], conv_w)).astype(f32)
    q_a = _l2n(qkv_a[..., :nqk].reshape(b, s, DN_HEADS, DN_DK))
    k_a = _l2n(qkv_a[..., nqk:2 * nqk].reshape(b, s, DN_HEADS, DN_DK))
    v_a = qkv_a[..., 2 * nqk:].reshape(b, s, DN_HEADS, DN_DV)
    z_a = proj[..., A_QKV1:A_Z1].astype(f32)
    beta = jax.nn.sigmoid(proj[..., A_Z1:A_B1].astype(f32))
    g = -jnp.exp(a_log.astype(f32)) * jax.nn.softplus(proj[..., A_B1:A_A1].astype(f32)
                                                       + dt_bias.astype(f32))
    o_a = _gated_delta_rule(q_a, k_a, v_a, g, beta)
    o_a = _rms(o_a, dn_out_gain).reshape(b, s, DN_WIDTH) * jax.nn.silu(z_a)
    y_a = jnp.einsum('bsc,cd->bsd', o_a.astype(x.dtype), w_up_a)

    qkv_b = proj[..., A_A1:B_QKV1].astype(f32).reshape(b, s, 3, SB_HEADS, SB_DH)
    q_b = jnp.swapaxes(_rms(qkv_b[:, :, 0], sb_q_gain), 1, 2)
    k_b = jnp.swapaxes(_rms(qkv_b[:, :, 1], sb_k_gain), 1, 2)
    v_b = jnp.swapaxes(qkv_b[:, :, 2], 1, 2)
    z_b = proj[..., B_QKV1:B_Z1].astype(f32)
    o_b = jnp.swapaxes(_stick_breaking(q_b, k_b, v_b), 1, 2).reshape(b, s, SB_WIDTH)
    o_b = o_b * jax.nn.silu(z_b)
    y_b = jnp.einsum('bsc,cd->bsd', o_b.astype(x.dtype), w_up_b)

    gates = jax.nn.sigmoid(proj[..., B_Z1:G1].astype(f32) + b_gate.astype(f32))
    merged = gates[..., :D_MODEL] * y_a.astype(f32) + gates[..., D_MODEL:] * y_b.astype(f32)
    return x + jnp.einsum('bsd,de->bse', merged.astype(x.dtype), w_out)

def second_inputs(seed: int = 0) -> dict:
    key = jax.random.key(seed)
    ks = jax.random.split(key, 14)
    f32 = jnp.float32
    nl = DEPTH
    nrm = jax.random.normal
    x = nrm(ks[0], (BATCH, SEQ, D_MODEL), f32)
    norm_gain = 1.0 + 0.02 * nrm(ks[1], (nl, D_MODEL), f32)
    w_in = nrm(ks[2], (nl, D_MODEL, PROJ_WIDTH), f32) * D_MODEL ** -0.5
    b_gate = 0.02 * nrm(ks[3], (nl, N_BRANCH * D_MODEL), f32)
    conv_w = nrm(ks[4], (nl, DN_CONV, A_QKV1), f32) * DN_CONV ** -0.5
    a_log = jnp.log(jax.random.uniform(ks[5], (nl, DN_HEADS), f32, minval=1.0, maxval=16.0))
    dt = jnp.exp(jax.random.uniform(ks[6], (nl, DN_HEADS), f32,
                                    minval=math.log(1e-3), maxval=math.log(1e-1)))
    dt_bias = dt + jnp.log(-jnp.expm1(-dt))
    dn_out_gain = 1.0 + 0.02 * nrm(ks[7], (nl, DN_DV), f32)
    sb_q_gain = 1.0 + 0.02 * nrm(ks[8], (nl, SB_DH), f32)
    sb_k_gain = 1.0 + 0.02 * nrm(ks[9], (nl, SB_DH), f32)
    w_up_a = nrm(ks[10], (nl, DN_WIDTH, D_MODEL), f32) * DN_WIDTH ** -0.5
    w_up_b = nrm(ks[11], (nl, SB_WIDTH, D_MODEL), f32) * SB_WIDTH ** -0.5
    w_out = nrm(ks[12], (nl, D_MODEL, D_MODEL), f32) * D_MODEL ** -0.5
    return {'x': x, 'norm_gain': norm_gain, 'w_in': w_in, 'b_gate': b_gate, 'conv_w': conv_w,
            'a_log': a_log, 'dt_bias': dt_bias, 'dn_out_gain': dn_out_gain,
            'sb_q_gain': sb_q_gain, 'sb_k_gain': sb_k_gain, 'w_up_a': w_up_a,
            'w_up_b': w_up_b, 'w_out': w_out}

def second_block(x, norm_gain, w_in, b_gate, conv_w, a_log, dt_bias, dn_out_gain,
              sb_q_gain, sb_k_gain, w_up_a, w_up_b, w_out):
    h = x
    for layer in range(DEPTH):
        h = _layer(h, norm_gain[layer], w_in[layer], b_gate[layer], conv_w[layer],
                   a_log[layer], dt_bias[layer], dn_out_gain[layer], sb_q_gain[layer],
                   sb_k_gain[layer], w_up_a[layer], w_up_b[layer], w_out[layer])
    return h


def setup_inputs(seed=0):
    out = dict(first_inputs(seed))
    for name, value in second_inputs(seed + 1).items():
        if name != "x":
            out[name + "_2"] = value
    return out


def reference(
    x, norm1_g, w_in, v_norm_g, w_s, b_s, q_norm_g, k_norm_g, lambda_q1, lambda_k1, lambda_q2,
    lambda_k2, sub_norm_g, w_up_a, w_up_b, w_gate, b_gate, w_out, norm2_g, w_rg, b_rg, w_re,
    b_re, w1, w3, w2, norm_gain_2, w_in_2, b_gate_2, conv_w_2, a_log_2, dt_bias_2,
    dn_out_gain_2, sb_q_gain_2, sb_k_gain_2, w_up_a_2, w_up_b_2, w_out_2,
):
    x = first_block(
        x, norm1_g, w_in, v_norm_g, w_s, b_s, q_norm_g, k_norm_g, lambda_q1, lambda_k1,
        lambda_q2, lambda_k2, sub_norm_g, w_up_a, w_up_b, w_gate, b_gate, w_out, norm2_g, w_rg,
        b_rg, w_re, b_re, w1, w3, w2,
    )
    return second_block(
        x, norm_gain_2, w_in_2, b_gate_2, conv_w_2, a_log_2, dt_bias_2, dn_out_gain_2,
        sb_q_gain_2, sb_k_gain_2, w_up_a_2, w_up_b_2, w_out_2,
    )


_drawn_inputs = setup_inputs


def setup_inputs(seed=0):
    import zlib

    import numpy as np

    out = dict(_drawn_inputs(seed))
    spreads = {}
    factors = {'v_norm_g': 3.841,
     'b_s': 3.051,
     'q_norm_g': 4.395,
     'k_norm_g': 2.943,
     'lambda_k1': 5.281,
     'lambda_q2': 5.657,
     'sub_norm_g': 4.047,
     'b_gate': 3.865,
     'b_rg': 6.009,
     'b_re': 4.889,
     'norm_gain_2': 5.877,
     'b_gate_2': 8.0,
     'dn_out_gain_2': 8.0,
     'sb_q_gain_2': 8.0,
     'sb_k_gain_2': 8.0}
    for name, (base, spread) in spreads.items():
        noise = np.random.default_rng([zlib.crc32(name.encode()), seed]).standard_normal(out[name].shape)
        drawn = base * np.exp(spread * noise) if base else spread * noise
        out[name] = __import__('jax').numpy.asarray(drawn.astype(out[name].dtype))
    for name, factor in factors.items():
        out[name] = (out[name] * factor).astype(out[name].dtype)
    return out
```

```python
from contextlib import ExitStack

import concourse.bass as bass
import concourse.mybir as mybir

F32 = mybir.dt.float32
F32R = mybir.dt.float32r
I32 = mybir.dt.int32
U32 = mybir.dt.uint32
ALU = mybir.AluOpType
ACT = mybir.ActivationFunctionType
AX_X = mybir.AxisListType.X

P = 128
BANKS = 8
BANK = 512
EPS = 1e-6
NEG = -1.0e30


class Queue:

    def __init__(self, sem):
        self.sem, self.count, self.steps, self.seen, self.last = sem, 0, [], {}, None

    def wait(self, *waits):
        for w in waits:
            if isinstance(w, list):
                self.wait(*w)
            elif w is not None and self.seen.get(w[0].name, 0) < w[1]:
                self.seen[w[0].name] = w[1]
                self.steps.append(lambda e, w=w: e.wait_ge(w[0], w[1]))

    def quiet(self, make, *waits):
        self.wait(*waits)
        self.steps.append(make)

    def do(self, make, *waits):
        self.wait(*waits)
        self.count += 1
        self.steps.append(lambda e: make(e).then_inc(self.sem, 1))
        self.last = (self.sem, self.count)
        return self.last

    def play(self, engine):
        for step in self.steps:
            step(engine)


class Arrivals:

    def __init__(self, sem):
        self.sem, self.count = sem, 0

    def start(self, queue, out, in_, *waits):
        queue.wait(*waits)
        self.count += 16
        queue.steps.append(lambda e: e.dma_start(out, in_).then_inc(self.sem, 16))
        return (self.sem, self.count)

    def start_indirect(self, queue, make, *waits):
        queue.wait(*waits)
        self.count += 16
        queue.steps.append(lambda e: make(e).then_inc(self.sem, 16))
        return (self.sem, self.count)


def build(nc, x, norm1_g, w_in, v_norm_g, w_s, b_s, q_norm_g, k_norm_g, lambda_q1, lambda_k1,
          lambda_q2, lambda_k2, sub_norm_g, w_up_a, w_up_b, w_gate, b_gate, w_out, norm2_g, w_rg,
          b_rg, w_re, b_re, w1, w3, w2, norm_gain_2, w_in_2, b_gate_2, conv_w_2, a_log_2,
          dt_bias_2, dn_out_gain_2, sb_q_gain_2, sb_k_gain_2, w_up_a_2, w_up_b_2, w_out_2, out,
          stop_at=None):
    ctx = ExitStack()
    sem = lambda name: ctx.enter_context(nc.semaphore(name))
    sb = lambda name, shape, dt=F32: ctx.enter_context(nc.sbuf_tensor(name, shape, dt))

    SEQ, D = x.shape[1], x.shape[2]
    NT = SEQ // P
    KD = D // P
    HB = 4
    UNIT = 2048
    G_A, DG = v_norm_g.shape[1], v_norm_g.shape[2]
    HEADS1, HD = 8, q_norm_g.shape[1]
    DV1 = 2 * HD
    LAM_INIT = 0.8 - 0.6 * 1.0
    NG, NE = w_rg.shape[2], w_re.shape[2]
    EPG = NE // NG
    DE = w1.shape[3]
    TOPK = 2
    CAP = 64
    EXTRA = (SEQ * TOPK) // (CAP + 1)
    SLOTS = (NE + EXTRA) * CAP
    DH, DK = a_log_2.shape[1], 128
    SBH, SBD = 8, sb_q_gain_2.shape[1]
    TAPS = conv_w_2.shape[1]
    CHUNK2 = 64

    xn_dram = nc.dram_tensor("xn_scratch", [SEQ, D], F32, kind="Internal").ap()
    y_dram = nc.dram_tensor("y_scratch", [SLOTS, D], F32, kind="Internal").ap()
    slot_dram = nc.dram_tensor("slot_scratch", [SLOTS, 2], F32, kind="Internal").ap()
    x2_dram = nc.dram_tensor("x2_scratch", [SEQ, D], F32, kind="Internal").ap()

    NR, NS = 3, 2
    raw = sb("raw", [P, NR, UNIT])
    whi = sb("whi", [P, NS, UNIT], F32R)
    wlo = sb("wlo", [P, NS, UNIT], F32R)
    hthi = sb("hthi", [P, KD, SEQ], F32R)
    htlo = sb("htlo", [P, KD, SEQ], F32R)
    yhi = sb("yhi", [P, KD, SEQ], F32R)
    ylo = sb("ylo", [P, KD, SEQ], F32R)
    m_all = sb("merged", [P, KD * SEQ])
    W = sb("work", [P, 4, UNIT])
    T = sb("scratch", [P, 5632])
    C = sb("consts", [P, 1536])
    SM = sb("smalls", [P, 2360])
    SI = sb("small_ints", [P, 128], I32)
    wba_r = sb("wba_r", [P, 2, KD * 2 * DH], F32R)
    PS = ctx.enter_context(nc.psum_tensor("PS", [P, BANKS, BANK], F32))

    pe, ve, ac, po, sp = (Queue(sem(n)) for n in ("s_pe", "s_ve", "s_ac", "s_po", "s_sp"))

    def mm(o, l, r, start, stop, *w, signal=False, part=False):
        make = lambda e: e.matmul(o, l, r, start=start, stop=stop, skip_group_check=part)
        return pe.do(make, *w) if signal else pe.quiet(make, *w)

    def turn(o, i, *w, signal=False):
        n = i.shape[0]
        make = lambda e: e.transpose(o, i, ident[0:n, 0:n])
        return pe.do(make, *w) if signal else pe.quiet(make, *w)

    def act(o, i, f, *w, bias=0.0, scale=1.0, acc=None):
        if acc is None:
            return ac.do(lambda e: e.activation(o, i, f, bias=bias, scale=scale), *w)
        return ac.do(lambda e: e.activation(o, i, f, bias=bias, scale=scale, accum_out=acc), *w)

    def tt(o, a, b, op, *w, q=None):
        return (q or ve).do(lambda e: e.tensor_tensor(o, a, b, op), *w)

    def ts(o, a, s1, s2, op0, op1, *w):
        if s2 is None:
            return ve.do(lambda e: e.tensor_scalar(o, a, s1, None, op0), *w)
        return ve.do(lambda e: e.tensor_scalar(o, a, s1, s2, op0, op1), *w)

    def stt(o, a, s, b, op0, op1, *w):
        return ve.do(lambda e: e.scalar_tensor_tensor(o, a, s, b, op0, op1), *w)

    def cp(o, a, *w):
        return ve.do(lambda e: e.tensor_copy(o, a), *w)

    def red(o, a, op, *w, neg=False):
        return ve.do(lambda e: e.tensor_reduce(o, a, AX_X, op, negate=neg), *w)

    MUL, ADD, SUB, MAX, MIN = ALU.mult, ALU.add, ALU.subtract, ALU.max, ALU.min

    def bc(ap, shape):
        return ap.unsqueeze(len(ap.shape)).broadcast_to(shape)

    def as_f32(ap):
        return ap.bitcast(F32)

    bank_free = [None] * BANKS
    bank_at = [0]

    def bank():
        while bank_free[bank_at[0] % BANKS] == "held":
            bank_at[0] += 1
        b = bank_at[0] % BANKS
        bank_at[0] += 1
        free, bank_free[b] = bank_free[b], "held"
        return b, PS[:, b, :], free

    sm_at = [0]

    def small(*shape):
        n = 1
        for s in shape:
            n *= s
        a = SM[:, sm_at[0]:sm_at[0] + n]
        sm_at[0] += n
        assert sm_at[0] <= 2360, sm_at
        return a if len(shape) == 1 else a.rearrange(
            "p (a b) -> p a b", b=shape[1]) if len(shape) == 2 else a.rearrange(
            "p (a b c) -> p a b c", b=shape[1], c=shape[2])

    c_at = [0]

    def const(n):
        a = C[:, c_at[0]:c_at[0] + n]
        c_at[0] += n
        assert c_at[0] <= 1536
        return a

    ident, ones, upper = const(P), const(P), const(P)
    t = po.do(lambda e: e.memset(ident, 0.0))
    t = po.do(lambda e: e.affine_select(out=ident, in_=ident, compare_op=ALU.not_equal, fill=1.0,
                                        base=0, pattern=[[-1, P]], channel_multiplier=1), t)
    ident_ok = t
    t = po.do(lambda e: e.memset(ones, 1.0))
    ones_ok = t
    t = po.do(lambda e: e.affine_select(out=upper, in_=ones, compare_op=ALU.is_gt, fill=0.0,
                                        base=0, pattern=[[1, P]], channel_multiplier=-1), t)
    const_ok = t

    vec_in = Arrivals(sem("s_vec"))
    vrows = sb("vector_rows", [P, P])
    vcols = const(P)
    v_at, vec_tok = [0], [None]
    vr_ok = ve.do(lambda e: e.memset(vrows[:, :], 0.0))

    def columns(ap, n):
        at = v_at[0]
        vec_tok[0] = vec_in.start(sp, vrows[at:at + n, :], ap, vr_ok)
        v_at[0] += n
        return vcols[:, at:at + n]

    g1 = columns(norm1_g[0].rearrange("(k p) -> k p", p=P), KD)
    gv = columns(v_norm_g[0], G_A)
    bg = columns(b_gate[0].rearrange("(k p) -> k p", p=P), 2 * KD)
    g2 = columns(norm2_g[0].rearrange("(k p) -> k p", p=P), KD)
    g3 = columns(norm_gain_2[0].rearrange("(k p) -> k p", p=P), KD)
    bg2 = columns(b_gate_2[0].rearrange("(k p) -> k p", p=P), 2 * KD)
    sg = columns(sub_norm_g, 1)
    dng = columns(dn_out_gain_2, 1)
    cw = columns(conv_w_2[0].rearrange("k (c p) -> (k c) p", p=P), 12 * TAPS).rearrange(
        "p (k c) -> p c k", k=TAPS)
    halves = {}
    for name, g in (("q1", q_norm_g), ("k1", k_norm_g), ("q2", sb_q_gain_2), ("k2", sb_k_gain_2)):
        at = v_at[0]
        for half in range(2):
            vec_tok[0] = vec_in.start(sp, vrows[at:at + 1, 64 * half:64 * half + 64], g, vr_ok)
        halves[name] = vcols[:, at:at + 1]
        v_at[0] += 1
    assert v_at[0] <= P
    g2p = small(KD)
    vec_tok[0] = vec_in.start(sp, g2p, norm2_g[0].rearrange("(p k) -> p k", k=KD))
    rows = {}

    def row(name, ap, n):
        a = small(n)[0:1, :]
        vec_tok[0] = vec_in.start(sp, a, ap)
        rows[name] = a

    for name, v in (("lq1", lambda_q1), ("lk1", lambda_k1), ("lq2", lambda_q2), ("lk2", lambda_k2)):
        row(name, v, HD)
    router_bias = small(NG + NE)[0:1, :]
    vec_in.start(sp, router_bias[:, 0:NG], b_rg)
    vec_in.start(sp, router_bias[:, NG:], b_re)
    row("alog", a_log_2, DH)
    row("dtb", dt_bias_2, DH)
    b, ps, bf = bank()
    tk = pe.do(lambda e: e.transpose(PS[:, 0, 0:P], vrows[:, :], ident), vec_tok[0], ident_ok)
    bank_free[b] = vecs = [cp(vcols, ps[:, 0:P], tk), vec_tok[0]]

    units = []

    def matrix(src, rows_, c0):
        for r in range(rows_ // BANK):
            units.append([(lambda a: a.rearrange("p (k n) -> p k n", k=HB),
                           src[r * BANK:(r + 1) * BANK, c0:c0 + BANK].rearrange("(k p) n -> p k n", p=P))])

    W_IN, W_G, A_W = w_in[0], w_gate[0], D
    for b in range(2):
        matrix(W_IN, D, A_W + BANK * b)
        matrix(W_IN, D, BANK * b)
    for b in range(2):
        matrix(W_G, D, BANK * b)
    for b in range(2):
        matrix(w_up_a[0], D, BANK * b)
    for b in range(2):
        for base in (2 * D, 3 * D, 4 * D):
            matrix(W_IN, D, base + BANK * b)
    for b in range(2):
        matrix(W_G, D, D + BANK * b)
    for b in range(2):
        matrix(w_up_b[0], D, BANK * b)
    for b in range(2):
        matrix(w_out[0], D, BANK * b)

    def expert_up(e):
        for kh in range(2):
            units.append([
                (lambda a, j=j: a.rearrange("p (j k f) -> p j k f", j=2, k=HB)[:, j],
                 w[0, e].rearrange("(p k) f -> p k f", k=KD)[:, HB * kh:HB * kh + HB, :])
                for j, w in enumerate((w1, w3))])

    def expert_down(e):
        units.append([(lambda a: a.rearrange("p (k n) -> p k n", k=2),
                       w2[0, e].rearrange("(p k) n -> p k n", k=2))])

    for e in range(NE + 1):
        if e < NE:
            expert_up(e)
        if e:
            expert_down(e - 1)
    W_IN2 = w_in_2[0]
    NH = DH * DK
    Z_A, B_A = 3 * NH, 4 * NH
    QKV_B = B_A + 2 * DH
    Z_B = QKV_B + 3 * SBH * SBD
    G_2 = Z_B + SBH * SBD
    for b in range(3):
        matrix(W_IN2, D, BANK * b)
    matrix(W_IN2, D, Z_A)
    matrix(W_IN2, D, Z_B)
    for b in range(3):
        matrix(W_IN2, D, QKV_B + BANK * b)
    for b in range(2):
        matrix(W_IN2, D, G_2 + BANK * b)
    for b in range(2):
        matrix(w_up_a_2[0], NH, BANK * b)
    for b in range(2):
        matrix(W_IN2, D, G_2 + D + BANK * b)
    for b in range(2):
        matrix(w_up_b_2[0], SBH * SBD, BANK * b)
    for b in range(2):
        matrix(w_out_2[0], D, BANK * b)

    raw_in = [Arrivals(sem(f"s_raw{i}")) for i in range(NR)]
    raw_free = [None] * NR
    split_free = [None] * NS
    split_ok = {}
    loaded, split = [0], [0]
    raw_tok = {}

    def load_more(upto):
        while loaded[0] < min(upto, len(units)):
            j = loaded[0]
            s = j % NR
            for place, src in units[j]:
                raw_tok[j] = raw_in[s].start(sp, place(raw[:, s, :]), src, raw_free[s])
            raw_free[s] = "held"
            loaded[0] += 1

    def split_more(upto):
        while split[0] < min(upto, len(units)):
            j = split[0]
            load_more(j + 1)
            r, s = j % NR, j % NS
            free = split_free[s]
            assert free != "held"
            hi = act(whi[:, s, :], raw[:, r, :], ACT.Copy, raw_tok[j], free)
            lo = tt(wlo[:, s, :], raw[:, r, :], as_f32(whi[:, s, :]), SUB, raw_tok[j], free, hi)
            split_ok[j] = [hi, lo]
            raw_free[r] = [hi, lo]
            split_free[s] = "held"
            split[0] += 1
            load_more(j + NR + 1)

    unit_at = [0]

    def take():
        j = unit_at[0]
        unit_at[0] += 1
        split_more(j + 1)
        return j, whi[:, j % NS, :], wlo[:, j % NS, :], split_ok[j]

    def done(j, tok):
        split_free[j % NS] = tok
        split_more(j + NS + 1)

    load_more(NR)

    def passes(o, lh, ll, rh, rl, start, stop, *w, signal=False):
        mm(o, lh, rh, start, False, *w)
        mm(o, lh, rl, False, False)
        return mm(o, ll, rh, False, stop, signal=signal)

    def product(turned, hi, lo, kt, ready, evac, between=None):
        held = [bank() for _ in range(HB)]
        tok = [None] * HB
        for kh in range(kt // HB):
            j, wh, wl, ok = take()
            wh, wl = (a.rearrange("p (k n) -> p k n", k=HB) for a in (wh, wl))
            for c in range(HB):
                cols = slice(c * P, c * P + P)
                for k in range(HB):
                    kk = kh * HB + k
                    if turned:
                        l, r = (wh[:, k, cols], wl[:, k, cols]), (hi[:, kk, :], lo[:, kk, :])
                    else:
                        l, r = (hi[:, kk, cols], lo[:, kk, cols]), (wh[:, k, :], wl[:, k, :])
                    last = kk == kt - 1
                    w = [ok, ready, held[c][2]] if k == 0 else []
                    end = passes(held[c][1], *l, *r, kk == 0, last, *w, signal=k == HB - 1)
                tok[c] = end
            done(j, end)
        if between:
            between()
        for c in range(HB):
            bank_free[held[c][0]] = evac(c, held[c][1], tok[c])

    rms_tmp = small(4 * 32)

    def inverse_rms(ss, n, count, ready, eps=EPS):
        v, l, y, h = (rms_tmp[:, i * 32:i * 32 + n] for i in range(4))
        r = small(n)
        return inverse_rms_in(v, l, y, h, r, ss, count, ready, eps)

    def inverse_rms_in(v, l, y, h, r, ss, count, ready, eps=EPS):
        tv = ts(v, ss, 1.0 / count, eps, MUL, ADD, ready)
        tl = act(l, v, ACT.Ln, tv)
        ty = act(y, l, ACT.Exp, tl, scale=-0.5)
        t = stt(h, y, -0.5, y, MUL, MUL, ty)
        t = tt(h, h, v, MUL, t)
        return r, stt(r, h, 1.5, y, ADD, MUL, t)

    def normalise(src, ready, free, gains, keep=None):
        ss = small(NT)
        xs = W[:, 0:2, :].rearrange("p a n -> p (a n)").rearrange("p (i d) -> p i d", i=NT)
        s = src.rearrange("p (i d) -> p i d", i=NT)
        for i in range(NT):
            t = act(xs[:, i, :], s[:, i, :], ACT.Square, ready, free, acc=ss[:, i:i + 1])
        r, rt = inverse_rms(ss, NT, D, t)
        toks = [ts(xs[:, i, :], s[:, i, :], r[:, i:i + 1], None, MUL, None, rt, t) for i in range(NT)]
        for k in range(KD):
            b, ps, bf = bank()
            for i in range(NT):
                tk = turn(ps[:, i * P:i * P + P], xs[:, i, k * P:k * P + P], toks, bf, ident_ok,
                          signal=i == NT - 1)
            if keep is not None:
                bank_free[b] = ts(keep[:, k, :], ps, gains[:, k:k + 1], None, MUL, None, tk, vecs)
                t2 = bank_free[b]
                continue
            h = act(hthi[:, k, :], ps, ACT.Copy, tk, vecs, free, scale=gains[:, k:k + 1])
            t2 = bank_free[b] = stt(htlo[:, k, :], ps, gains[:, k:k + 1], as_f32(hthi[:, k, :]),
                                    MUL, SUB, h)
        return toks, t2, tk

    def split_act(hi_o, lo_o, src, *w):
        h = act(hi_o, src, ACT.Copy, *w)
        return tt(lo_o, src, as_f32(hi_o), SUB, h)

    x_in = Arrivals(sem("s_x"))
    xv = x.rearrange("b (i p) d -> p (b i) d", p=P)
    x_ok = x_in.start(sp, m_all[:, :].rearrange("p (i d) -> p i d", i=NT), xv)
    _, ht_ok, _ = normalise(m_all[:, :], x_ok, None, g1)
    x_read = ve.last

    zrows = T[0:EXTRA * CAP // 8, 4608:4608 + D]
    t = po.do(lambda e: e.memset(zrows, 0.0))
    yz = Arrivals(sem("s_yzero"))
    for n in range(8):
        yz_ok = yz.start(po, y_dram[NE * CAP:, :].rearrange("(n p) d -> n p d", n=8)[n], zrows, t)

    ws_in = Arrivals(sem("s_ws"))
    wsn = W[:, 3, 0:1024].rearrange("p (g s) -> p g s", g=G_A)
    wst = T[:, 0:1024].rearrange("p (g s) -> p g s", g=G_A)
    bsb = T[:, 1024:2048]
    bsrow = T[0:1, 2048:3072]
    ws_in.start(sp, wsn, w_s[0].rearrange("g t s -> t g s"))
    ws_ok = ws_in.start(sp, bsrow, b_s[0:1].rearrange("o g t -> o (g t)"))
    t = po.do(lambda e: e.affine_select(out=wsn, in_=wsn, compare_op=ALU.is_ge, fill=0.0, base=0,
                                        pattern=[[0, G_A], [-1, P]], channel_multiplier=1), ws_ok)
    for half in range(2):
        b, ps, bf = bank()
        for g in range(4):
            tk = turn(ps[:, g * P:g * P + P], wsn[:, half * 4 + g, :], t, bf, signal=g == 3)
        bank_free[b] = wst_ok = cp(wst[:, half * 4:half * 4 + 4, :], ps.rearrange("p (g s) -> p g s", g=4), tk)
        b, ps, bf = bank()
        tk = mm(ps, ones[0:1, :], bsrow[:, half * BANK:half * BANK + BANK], True, True, ws_ok,
                ones_ok, bf, signal=True)
        bank_free[b] = bsb_ok = cp(bsb[:, half * BANK:half * BANK + BANK], ps, tk)

    def group_norm(dst, squares, width, ready):
        n = UNIT // width
        ss = small(n)
        ts_ = red(ss, squares.rearrange("p (g d) -> p g d", d=width), ADD, ready)
        r, rt = inverse_rms(ss, n, width, ts_)
        d = dst.rearrange("p (g d) -> p g d", d=width)
        return tt(d, d, bc(r, [P, n, width]), MUL, rt)

    def natural_block(dst, squares, free, sq_free=None):
        toks = []

        def evac(c, ps, tok):
            o = dst.rearrange("p (i n) -> p i n", i=NT)[:, c, :]
            if squares is None:
                toks.append(act(o, ps, ACT.Copy, tok, free))
                return toks[-1]
            a = act(o, ps, ACT.Copy, tok, free)
            toks.append(act(squares.rearrange("p (i n) -> p i n", i=NT)[:, c, :], o, ACT.Square, a, sq_free))
            return a
        product(False, hthi, htlo, KD, ht_ok, evac)
        return toks

    w_free = [[wst_ok, ve.last]] * 4
    y_ok = []
    spat_tmp = T[:, 3072:3072 + 2 * BANK].rearrange("p (a n) -> p a n", a=2)
    for b in range(2):
        vt = natural_block(W[:, 0, :], W[:, 2, :], w_free[0], w_free[2])
        vn_ok = group_norm(W[:, 0, :], W[:, 2, :], DG, vt)
        ut = W[:, 1, :].rearrange("p (c n) -> p c n", c=HB)
        u_ok = {}

        def evac_u(c, ps, tok):
            u_ok[c] = act(ut[:, c, :], ps, ACT.Copy, tok, w_free[1])
            return u_ok[c]
        product(True, hthi, htlo, KD, ht_ok, evac_u)
        vn = W[:, 0, :].rearrange("p (i n) -> p i n", i=NT)
        for g in range(4):
            gg = b * 4 + g
            bb, ps, bf = bank()
            for i in range(NT):
                tk = mm(ps[:, i * P:i * P + P], vn[:, i, g * P:g * P + P], wst[:, gg, :], True, True,
                        vn_ok, wst_ok, bf, signal=i == NT - 1)
            tmp = spat_tmp[:, g % 2, :]
            t = stt(tmp.rearrange("p (i s) -> p i s", i=NT), ps.rearrange("p (i s) -> p i s", i=NT),
                    gv[:, gg:gg + 1], bsb[:, gg * P:gg * P + P].unsqueeze(1).broadcast_to([P, NT, P]),
                    MUL, ADD, tk, bsb_ok, vecs, y_ok[-2:])
            bank_free[bb] = t
            t = tt(tmp, tmp, ut[:, g, :], MUL, t, u_ok[g])
            u_read = t
            y_ok.append(split_act(yhi[:, gg, :], ylo[:, gg, :], tmp, t))
        w_free = [tk, u_read, vn_ok, None]

    mg = m_all[:, :].rearrange("p (k n) -> p k n", k=KD)

    def gates(bias, c0, free):
        g = W[:, 0:2, :].rearrange("p a n -> p (a n)").rearrange("p (k n) -> p k n", k=KD)
        ok = []
        for b in range(2):
            def evac(c, ps, tok):
                k = b * HB + c
                ok.append(act(g[:, k, :], ps, ACT.Sigmoid, tok, free, vecs, bias=bias[:, c0 + k:c0 + k + 1]))
                return ok[-1]
            product(True, hthi, htlo, KD, ht_ok, evac)
        return g, ok

    def merge_first(hi, lo, kt, ready, g, g_ok, free):
        for b in range(2):
            def evac(c, ps, tok):
                k = b * HB + c
                return tt(mg[:, k, :], ps, g[:, k, :], MUL, tok, g_ok, free)
            product(True, hi, lo, kt, ready, evac)
        return ve.last

    merge_tmp = T[:, 4608:4608 + 2 * BANK].rearrange("p (a n) -> p a n", a=2)

    def merge_second(hi, lo, kt, ready, g, g_ok, free):
        ok = []
        for b in range(2):
            def evac(c, ps, tok):
                k = b * HB + c
                tmp = merge_tmp[:, k % 2, :]
                f = tt(tmp, ps, g[:, k, :], MUL, tok, g_ok, free, ok[-2:])
                t = tt(mg[:, k, :], mg[:, k, :], tmp, ADD, f)
                ok.append(split_act(hthi[:, k, :], htlo[:, k, :], mg[:, k, :], t))
                return f
            product(True, hi, lo, kt, ready, evac)
        return ok

    g, g_ok = gates(bg, 0, w_free)
    m_ok = merge_first(yhi, ylo, KD, y_ok, g, g_ok, x_read)
    y_free = pe.last

    lam1 = small(2)
    lt = small(HD)[0:1, :]
    for n, (a, c) in enumerate((("lq1", "lk1"), ("lq2", "lk2"))):
        t = tt(lt, rows[a], rows[c], MUL, vecs, ve.last)
        t = red(lam1[0:1, n:n + 1], lt, ADD, t)
    lam2 = small(2)
    t = act(lam2[0:1, :], lam1[0:1, :], ACT.Exp, t)
    lam3 = small(1)
    t = tt(lam3[0:1, :], lam2[0:1, 1:2], lam2[0:1, 0:1], SUB, t)
    t = ts(lam3[0:1, :], lam3[0:1, :], -LAM_INIT, None, ADD, None, t)
    nlam = small(1)
    b, ps, bf = bank()
    tk = mm(ps[:, 0:1], ones[0:1, :], lam3[0:1, :], True, True, t, bf, signal=True)
    bank_free[b] = nlam_ok = cp(nlam, ps[:, 0:1], tk)
    sg8 = small(1)
    sg_ok = ts(sg8, sg, 1.0 - LAM_INIT, None, MUL, None, vecs)
    gq8 = {}
    for name in ("q1", "q2"):
        a = small(1)
        gq_ok = ts(a, halves[name], HD ** -0.5, None, MUL, None, vecs)
        gq8[name] = a

    dist = T[:, 0:BANK]
    spat_read = [y_ok[-1], pe.last, ve.last]
    dist_i = W[:, 3, 0:BANK].bitcast(I32)
    t = po.do(lambda e: e.iota(dist_i, pattern=[[1, BANK]], base=-(SEQ - P), channel_multiplier=-1), spat_read)
    t = cp(dist, dist_i, t, spat_read)
    dist_ok = po.do(lambda e: e.affine_select(out=dist, in_=dist, compare_op=ALU.is_ge, fill=NEG,
                                              base=SEQ - P, pattern=[[-1, BANK]], channel_multiplier=1), t)

    def turn_block(src, dst, gain, ready, free):
        s = src.rearrange("p (i n) -> p i n", i=NT)
        d = dst.rearrange("p (c n) -> p c n", c=HB)
        for c in range(HB):
            b, ps, bf = bank()
            for i in range(NT):
                tk = turn(ps[:, i * P:i * P + P], s[:, i, c * P:c * P + P], ready, bf, signal=i == NT - 1)
            t = bank_free[b] = act(d[:, c, :], ps, ACT.Copy, tk, free, gq_ok, vecs, scale=gain)
        return t, tk

    S_ = T[:, 512:512 + 2048].rearrange("p (u c n) -> p u c n", u=2, c=2)
    AT = T[:, 2560:2560 + 1024].rearrange("p (u n) -> p u n", u=2)
    BI = T[:, 3584:3584 + 512]
    ON = T[:, 4096:4096 + 512]
    ON2 = T[:, 4608:4608 + 1024].rearrange("p (u n) -> p u n", u=2)
    w_free = [g_ok, g_ok, None, dist_ok]
    g_read = m_ok
    q_free = k_free = v_free = [g_read, dist_ok]
    yb_ok = []
    s_free, at_free, bi_free, on_free = [None] * 2, [None] * 2, None, yz_ok
    ring2 = small(2, 16)
    n_it = 0
    nat_free = [g_read, dist_ok, t]
    for b in range(2):
        qt, kt_ = W[:, 1, :], W[:, 2, :]
        vt = natural_block(W[:, 0, :], W[:, 3, :], nat_free, nat_free)
        n_ok = group_norm(W[:, 0, :], W[:, 3, :], HD, vt)
        q_ok, rd = turn_block(W[:, 0, :], qt, gq8["q1"], n_ok, q_free)
        vt = natural_block(W[:, 0, :], W[:, 3, :], [rd, n_ok], [n_ok])
        n_ok = group_norm(W[:, 0, :], W[:, 3, :], HD, vt)
        k_ok, rd = turn_block(W[:, 0, :], kt_, halves["k1"], n_ok, k_free)
        v_ok = natural_block(W[:, 0, :], None, [rd, n_ok])
        qT = qt.rearrange("p (c n) -> p c n", c=HB)
        kT = kt_.rearrange("p (c n) -> p c n", c=HB)
        vN = W[:, 0, :].rearrange("p (i n) -> p i n", i=NT)
        for h in range(4):
            hh = b * 4 + h
            bi_ok = ts(BI, dist, 2.0 ** (-8.0 * (hh + 1) / HEADS1), None, MUL, None, dist_ok, bi_free)
            ob, ops, obf = bank()
            for i in range(NT):
                u = n_it % 2
                n_it += 1
                n = P * (i + 1)
                sm = ring2[:, u, :]
                held = [bank(), bank()]
                sc_t = []
                for c in range(2):
                    tk = mm(held[c][1][:, 0:n], qT[64 * c:64 * c + 64, h, i * P:i * P + P],
                            kT[64 * c:64 * c + 64, h, 0:n], True, True, q_ok, k_ok, held[c][2], signal=True)
                    t = tt(S_[:, u, c, 0:n], held[c][1][:, 0:n], BI[:, BANK - n:BANK], ADD, tk, bi_ok, s_free[u])
                    bank_free[held[c][0]] = t
                    bi_free = t
                t = red(sm[:, 0:2], S_[:, u, :, 0:n], MAX, t, neg=True)
                for c in range(2):
                    te = act(S_[:, u, c, 0:n], S_[:, u, c, 0:n], ACT.Exp, t, bias=sm[:, c:c + 1], acc=sm[:, 2 + c:3 + c])
                t = ve.do(lambda e, sm=sm: e.reciprocal(sm[:, 4:6], sm[:, 2:4]), te)
                t = tt(sm[:, 6:7], sm[:, 5:6], nlam, MUL, t, nlam_ok)
                t = ts(S_[:, u, 1, 0:n], S_[:, u, 1, 0:n], sm[:, 6:7], None, MUL, None, t)
                t = stt(S_[:, u, 0, 0:n], S_[:, u, 0, 0:n], sm[:, 4:5], S_[:, u, 1, 0:n], MUL, ADD, t)
                bb, ps, bf = bank()
                for k in range(i + 1):
                    tk = turn(ps[:, k * P:k * P + P], S_[:, u, 0, k * P:k * P + P], t, bf, signal=k == i)
                s_free[u] = tk
                t = bank_free[bb] = act(AT[:, u, 0:n], ps[:, 0:n], ACT.Copy, tk, at_free[u])
                for k in range(i + 1):
                    tk = mm(ops[:, i * P:i * P + P], AT[:, u, k * P:k * P + P], vN[:, k, h * P:h * P + P],
                            k == 0, k == i, t, v_ok, obf, signal=k == i)
                at_free[u] = tk
            o3 = ops.rearrange("p (i n) -> p i n", i=NT)
            sq = ON2[:, 0, :].rearrange("p (i n) -> p i n", i=NT)
            ssn = small(NT)
            t = act(sq, o3, ACT.Square, tk, on_free)
            t = red(ssn, sq, ADD, t)
            r, rt = inverse_rms(ssn, NT, DV1, t)
            t = bank_free[ob] = tt(ON.rearrange("p (i n) -> p i n", i=NT), o3, bc(r, [P, NT, P]), MUL, rt, on_free)
            bb, ps, bf = bank()
            for i in range(NT):
                on_free = turn(ps[:, i * P:i * P + P], ON[:, i * P:i * P + P], t, bf, signal=i == NT - 1)
            th = act(yhi[:, hh, :], ps, ACT.Copy, on_free, y_free, sg_ok, scale=sg8)
            t = bank_free[bb] = stt(ylo[:, hh, :], ps, sg8, as_f32(yhi[:, hh, :]), MUL, SUB, th)
            yb_ok.append(t)
        nat_free = pe.last
        q_free = k_free = pe.last

    g, g_ok = gates(bg, KD, pe.last)
    parts = merge_second(yhi, ylo, KD, yb_ok, g, g_ok, m_ok)
    xw = W[:, 2:4, :].rearrange("p a n -> p (a n)").rearrange("p (i d) -> p i d", i=NT)
    x_ok = x_in.start(sp, xw, xv, pe.last, ve.last)
    x1 = m_all[:, :].rearrange("p (i d) -> p i d", i=NT)
    for b in range(2):
        def evac(c, ps, tok):
            cols = slice(b * BANK, b * BANK + BANK)
            return tt(x1[:, c, cols], ps, xw[:, c, cols], ADD, tok, x_ok, parts)
        product(False, hthi, htlo, KD, parts, evac)
    x1_ok = ve.last

    h2t = W[:, 2:4, :].rearrange("p a n -> p (a n)").rearrange("p (k n) -> p k n", k=KD)
    xs_toks, h2_ok, xs_read = normalise(m_all[:, :], x1_ok, [x1_ok, pe.last], g2, keep=h2t)
    xs = W[:, 0:2, :].rearrange("p a n -> p (a n)").rearrange("p (i d) -> p i d", i=NT)
    xn_out = Arrivals(sem("s_xn"))
    xn_ok = xn_out.start(sp, xn_dram.rearrange("(i p) d -> p i d", p=P), xs, xs_toks)
    wr = T[:, 0:KD * (NG + NE)].rearrange("p (k n) -> p k n", k=KD)
    wr_in = Arrivals(sem("s_wr"))
    t_free = [ve.last, pe.last, ac.last]
    wr_in.start(sp, wr[:, :, 0:NG], w_rg[0].rearrange("(k p) n -> p k n", p=P), t_free)
    wr_ok = wr_in.start(sp, wr[:, :, NG:], w_re[0].rearrange("(k p) n -> p k n", p=P))
    b, ps, bf = bank()
    lgp = ps.rearrange("p (i n) -> p i n", i=NT)
    for i in range(NT):
        for k in range(KD):
            mm(lgp[:, i, 0:NG + NE], h2t[:, k, i * P:i * P + P], wr[:, k, :], k == 0, False,
               h2_ok, wr_ok, bf)
        tk = mm(lgp[:, i, 0:NG + NE], ones[0:1, :], router_bias, False, True, vecs, signal=True)
    tcur = [T.shape[1] - 5632 + 512]

    def tmp_(*shape):
        n = 1
        for s_ in shape:
            n *= s_
        a = T[:, tcur[0]:tcur[0] + n]
        tcur[0] += n
        assert tcur[0] <= 5632
        if len(shape) == 2:
            return a.rearrange("p (a b) -> p a b", b=shape[1])
        if len(shape) == 3:
            return a.rearrange("p (a b c) -> p a b c", b=shape[1], c=shape[2])
        return a

    h2t_read = tk
    lg = tmp_(NT, NG + NE)
    t = bank_free[b] = cp(lg, lgp[:, :, 0:NG + NE], tk, t_free)
    iot_i = SI[:, 0:NE]
    eidx = tmp_(NE)
    ti = po.do(lambda e: e.iota(iot_i, pattern=[[1, NE]], base=0, channel_multiplier=0))
    t = cp(eidx, iot_i, ti, t)

    def first_of(values, best, n, tok):
        oh, rk, bk = tmp_(NT, n), tmp_(NT, n), tmp_(NT)
        t = tt(oh, values, bc(best, [P, NT, n]), ALU.is_equal, tok)
        w8 = tmp_(n)
        t = ts(w8, eidx[:, 0:n], -1.0, float(n), MUL, ADD, t)
        t = tt(rk, oh, w8.unsqueeze(1).broadcast_to([P, NT, n]), MUL, t)
        t = red(bk, rk, MAX, t)
        return oh, tt(oh, rk, bc(bk, [P, NT, n]), ALU.is_equal, t)

    mx = tmp_(NT)
    t = red(mx, lg[:, :, 0:NG], MAX, t)
    ohg, t = first_of(lg[:, :, 0:NG], mx, NG, t)
    ex = tmp_(NT, NG)
    t = tt(ex, lg[:, :, 0:NG], bc(mx, [P, NT, NG]), SUB, t)
    t = act(ex, ex, ACT.Exp, t)
    gs, gate = tmp_(NT), tmp_(NT)
    t = red(gs, ex, ADD, t)
    t = ve.do(lambda e: e.reciprocal(gate, gs), t)
    sel = tmp_(NT, NE)
    for i in range(NT):
        t = tt(sel[:, i, :].rearrange("p (g e) -> p g e", g=NG), lg[:, i, NG:].rearrange("p (g e) -> p g e", g=NG),
               bc(ohg[:, i, :], [P, NG, EPG]), MUL, t)
    el = tmp_(NT, EPG)
    for i in range(NT):
        t = red(el[:, i, :], sel[:, i, :].rearrange("p (g e) -> p e g", g=NG), ADD, t)
    m1, m2 = tmp_(NT), tmp_(NT)
    t = red(m1, el, MAX, t)
    oh1, t = first_of(el, m1, EPG, t)
    el2 = tmp_(NT, EPG)
    t = stt(el2, oh1, NEG, el, MUL, ADD, t)
    t = red(m2, el2, MAX, t)
    oh2, t = first_of(el2, m2, EPG, t)
    wt = tmp_(2, NT)
    p2, den = tmp_(NT), tmp_(NT)
    t = tt(p2, m2, m1, SUB, t)
    t = act(p2, p2, ACT.Exp, t)
    t = ts(den, p2, 1.0, None, ADD, None, t)
    t = ve.do(lambda e: e.reciprocal(den, den), t)
    t = tt(wt[:, 0, :], den, gate, MUL, t)
    t = tt(wt[:, 1, :], wt[:, 0, :], p2, MUL, t)
    E = [tmp_(NT, NE), tmp_(NT, NE)]
    for n, oh in enumerate((oh1, oh2)):
        for i in range(NT):
            t = tt(E[n][:, i, :].rearrange("p (g e) -> p g e", g=NG),
                   ohg[:, i, :].unsqueeze(2).broadcast_to([P, NG, EPG]),
                   oh[:, i, :].unsqueeze(1).broadcast_to([P, NG, EPG]), MUL, t)
    both = tmp_(NT, NE)
    t = tt(both, E[0], E[1], ADD, t)
    b, ps, bf = bank()
    rp = ps[:, 0:(NT + 1) * NE].rearrange("p (i e) -> p i e", i=NT + 1)
    for i in range(NT + 1):
        for j in range(min(i + 1, NT)):
            last = j == min(i, NT - 1)
            tk = mm(rp[:, i, :], upper if j == i else ones, both[:, j, :], j == 0, last, t, const_ok, bf,
                    signal=last)
    rank, cnt = tmp_(NT, NE), tmp_(NE)
    t = cp(rank, rp[:, 0:NT, :], tk)
    t = bank_free[b] = cp(cnt, rp[:, NT, :], t)
    xtra, tmpe = tmp_(NE), tmp_(NE)
    MAXC = SEQ // CAP
    t = ts(xtra, cnt, float(CAP), None, ALU.is_gt, None, t)
    for m in range(2, MAXC):
        t = stt(xtra, cnt, float(CAP * m), xtra, ALU.is_gt, ADD, t)
    inc = [tmp_(NE), tmp_(NE)]
    t = cp(inc[0], xtra, t)
    cur, step = 0, 1
    while step < NE:
        t = cp(inc[1 - cur][:, 0:step], inc[cur][:, 0:step], t)
        t = tt(inc[1 - cur][:, step:], inc[cur][:, step:], inc[cur][:, 0:NE - step], ADD, t)
        cur, step = 1 - cur, 2 * step
    incl = inc[cur]
    off = tmp_(NE)
    t = tt(off, incl, xtra, SUB, t)
    slot = tmp_(2, NT)
    inf = tmp_(2 * NT, 2)
    toki = SI[:, 32:32 + NT]
    ti = po.do(lambda e: e.iota(toki, pattern=[[P, NT]], base=0, channel_multiplier=1))
    base0, base1 = tmp_(NE), tmp_(NE)
    t = ts(base0, eidx, float(CAP), None, MUL, None, t)
    t = ts(base1, off, float(CAP), float(CAP * (NE - 1)), MUL, ADD, t)
    prod, r1, a0, a1, far = tmp_(NT, NE), tmp_(NT), tmp_(NT), tmp_(NT), tmp_(NT)
    for n in range(2):
        for src, dst in ((rank, r1), (base0.unsqueeze(1).broadcast_to([P, NT, NE]), a0),
                         (base1.unsqueeze(1).broadcast_to([P, NT, NE]), a1)):
            t = tt(prod, E[n], src, MUL, t)
            t = red(dst, prod, ADD, t)
        t = ts(far, r1, float(CAP), None, ALU.is_ge, None, t)
        t = tt(a1, a1, a0, SUB, t)
        t = tt(a1, a1, far, MUL, t)
        t = tt(a0, a0, a1, ADD, t)
        t = tt(slot[:, n, :], a0, r1, ADD, t)
        t = cp(inf[:, n * NT:(n + 1) * NT, 0], toki, t, ti)
        t = cp(inf[:, n * NT:(n + 1) * NT, 1], wt[:, n, :], t)
    slot_u = SI[:, 40:40 + 2 * NT].bitcast(U32)
    slot_ok = cp(slot_u, slot.rearrange("p a b -> p (a b)"), t)
    ovf, ovn = tmp_(EXTRA, NE), tmp_(EXTRA)
    jrow_i = SI[:, 64:64 + EXTRA]
    jrow = tmp_(EXTRA)
    ti = po.do(lambda e: e.iota(jrow_i, pattern=[[1, EXTRA]], base=0, channel_multiplier=0))
    t = cp(jrow, jrow_i, ti, slot_ok)
    t = tt(ovf, incl.unsqueeze(1).broadcast_to([P, EXTRA, NE]), bc(jrow, [P, EXTRA, NE]), ALU.is_le, t)
    t = red(ovn, ovf, ADD, t)
    t = ts(ovn, ovn, float(NE - 1), None, MIN, None, t)
    ov_ids = SI[:, 80:80 + EXTRA + 1]
    t = cp(ov_ids[:, 0:EXTRA], ovn, t)
    ov_ok = cp(ov_ids[:, EXTRA:EXTRA + 1], incl[:, NE - 1:NE], t)

    zer = tmp_(SLOTS * 2 // CAP)[0:CAP]
    z_ok = ve.do(lambda e: e.memset(zer, 0.0), slot_ok)
    tab = Arrivals(sem("s_tab"))
    tab_ok = tab.start(po, slot_dram.rearrange("(p s) c -> p (s c)", p=CAP), zer, z_ok)
    scat = Arrivals(sem("s_scat"))
    for n in range(2 * NT):
        sc_ok = scat.start_indirect(po, lambda e, n=n: e.indirect_dma_start(
            out=slot_dram, out_offset=bass.IndirectOffsetOnAxis(ap=slot_u[:, n:n + 1], axis=0),
            in_=inf[:, n, :], in_offset=None), tab_ok, slot_ok)
    NTILE = NE + EXTRA
    info = tmp_(NTILE, 2)[0:CAP]
    idx = SI[0:CAP, 0:1]
    idx = sb("slot_tokens", [CAP, NTILE], U32)
    back = Arrivals(sem("s_back"))
    in_ok = back.start(po, info, slot_dram.rearrange("(n p) c -> p n c", p=CAP), sc_ok)
    idx_ok = cp(idx[:, :], info[:, :, 0], in_ok)

    XG = W[0:CAP, 0:2, :].rearrange("p a n -> p (a n)")[:, 0:3 * D].rearrange("p (u d) -> p u d", u=3)
    YO = W[0:CAP, 2, :].rearrange("p (u d) -> p u d", u=2)
    HF = T[:, 0:BANK].rearrange("p (k n) -> p k n", k=KD)
    HF = W[:, 3, 0:BANK].rearrange("p (k n) -> p k n", k=KD)
    SG = W[0:CAP, 3, 512:512 + 2 * DE].rearrange("p (u n) -> p u n", u=2)
    HID = W[0:CAP, 3, 1024:1024 + 2 * DE].rearrange("p (u n) -> p u n", u=2)
    GHI = yhi[:, 0:2, :].rearrange("p u (k n) -> p u k n", k=KD)
    GLO = ylo[:, 0:2, :].rearrange("p u (k n) -> p u k n", k=KD)
    HHI = yhi[:, 2, 0:4 * CAP].rearrange("p (u k n) -> p u k n", u=2, k=2)
    HLO = ylo[:, 2, 0:4 * CAP].rearrange("p (u k n) -> p u k n", u=2, k=2)
    xg_in = [Arrivals(sem(f"s_xg{i}")) for i in range(3)]
    y_out = [Arrivals(sem(f"s_yo{i}")) for i in range(2)]
    xg_ok, xg_free = {}, [[xs_read, xn_ok, ve.last]] * 3
    g_split, g_free, up_tok, hid_ok, h_free, yo_free = {}, [[y_free, pe.last]] * 2, {}, {}, [None] * 2, [None] * 2
    w_clear = [h2t_read, xn_ok]
    dk = [None]

    def gather(e):
        u = e % 3
        xg_ok[e] = xg_in[u].start_indirect(po, lambda q: q.indirect_dma_start(
            out=XG[:, u, :], out_offset=None, in_=xn_dram,
            in_offset=bass.IndirectOffsetOnAxis(ap=idx[:, e:e + 1], axis=0)), idx_ok, xg_free[u], xn_ok)

    def bring(e):
        u = e % 2
        b, ps, bf = bank()
        pv = ps.rearrange("p (k n) -> p k n", k=KD)
        for k in range(KD):
            tk = turn(pv[:, k, :], XG[:, e % 3, k::KD], xg_ok[e], bf, signal=k == KD - 1)
        xg_free[e % 3] = tk
        t = bank_free[b] = tt(HF, pv, bc(g2p, [P, KD, CAP]), MUL, tk, vecs, w_clear, dk[0])
        h = act(GHI[:, u], HF, ACT.Copy, t, g_free[u])
        dk[0] = h
        g_split[e] = tt(GLO[:, u], HF, as_f32(GHI[:, u]), SUB, h, g_free[u])

    def up(e):
        u = e % 2
        b, ps, bf = bank()
        for kh in range(2):
            j, wh, wl, ok = take()
            wh, wl = (a.rearrange("p (j k f) -> p j k f", j=2, k=HB) for a in (wh, wl))
            for k in range(HB):
                kk = kh * HB + k
                tk = passes(ps[0:CAP, :], GHI[:, u, kk, :], GLO[:, u, kk, :], wh[:, :, k, :], wl[:, :, k, :],
                            kk == 0, kk == KD - 1, ok, g_split[e], bf, signal=k == HB - 1)
            done(j, tk)
        g_free[u] = tk
        ta = act(SG[:, u, :], ps[0:CAP, 0:DE], ACT.Sigmoid, tk, h_free[u], w_clear)
        t = tt(SG[:, u, :], SG[:, u, :], ps[0:CAP, 0:DE], MUL, ta)
        t = stt(HID[:, u, :], SG[:, u, :], info[:, e, 1:2], ps[0:CAP, DE:2 * DE], MUL, MUL, t, h_free[u])
        bank_free[b] = hid_ok[e] = t

    def down(e):
        u = e % 2
        b, ps, bf = bank()
        pv = ps[:, 0:2 * CAP].rearrange("p (k n) -> p k n", k=2)
        for k in range(2):
            tk = turn(pv[:, k, :], HID[:, u, k::2], hid_ok[e], bf, signal=k == 1)
        h_free[u] = tk
        h = act(HHI[:, u], pv, ACT.Copy, tk)
        t = bank_free[b] = tt(HLO[:, u], pv, as_f32(HHI[:, u]), SUB, h)
        j, wh, wl, ok = take()
        wh, wl = (a.rearrange("p (k n) -> p k n", k=2) for a in (wh, wl))
        held = [bank(), bank()]
        toks = []
        for half in range(2):
            cols = slice(half * BANK, half * BANK + BANK)
            for k in range(2):
                tk = passes(held[half][1][0:CAP, :], HHI[:, u, k, :], HLO[:, u, k, :], wh[:, k, cols],
                            wl[:, k, cols], k == 0, k == 1, ok, t, held[half][2], signal=k == 1)
            toks.append(tk)
        done(j, tk)
        for half in range(2):
            cols = slice(half * BANK, half * BANK + BANK)
            t = bank_free[held[half][0]] = act(YO[:, u, cols], held[half][1][0:CAP, :], ACT.Copy,
                                               toks[half], yo_free[u], w_clear)
        yo_free[u] = y_out[u].start(ac, y_dram[e * CAP:(e + 1) * CAP, :], YO[:, u, :], t)

    gather(0)
    gather(1)
    bring(0)
    for e in range(NE + 1):
        if e < NE:
            if e + 2 < NE:
                gather(e + 2)
            up(e)
            if e + 1 < NE:
                bring(e + 1)
        if e:
            down(e - 1)

    main_end = [q.last for q in (pe, ve, ac, po)] + yo_free + [yz_ok]
    names = ("pe", "ve", "ac", "po", "sp")
    ope, ove, oac, opo, osp = (Queue(sem(f"s_over_{n}")) for n in names)
    o_in, o_w, o_y = (Arrivals(sem(f"s_over_{n}")) for n in ("in", "w", "y"))
    w13 = W[:, 0:2, :].rearrange("p a n -> p (a n)").rearrange("p (j k f) -> p j k f", j=2, k=KD)
    wdn = W[:, 2, :].rearrange("p (k n) -> p k n", k=2)
    oxg = W[0:CAP, 3, 0:D]
    ogt = W[:, 3, D:D + BANK].rearrange("p (k n) -> p k n", k=KD)
    osg = W[0:CAP, 3, D + BANK:D + BANK + DE]
    oht = W[:, 3, D + BANK + DE:D + BANK + DE + 2 * CAP].rearrange("p (k n) -> p k n", k=2)
    OVB = [PS[:, n, :] for n in range(4)]
    w_load = {}
    end = None
    for j in range(EXTRA):
        tile = NE + j
        def from_id(e, j=j):
            w_load[j] = e.value_load(ov_ids[0:1, j:j + 1], min_val=0, max_val=NE - 1)
        osp.quiet(from_id, end)
        for n, (dst, src) in enumerate(((w13[:, 0], w1), (w13[:, 1], w3), (wdn, w2))):
            osp.wait(end)
            o_w.count += 16
            def load(e, j=j, dst=dst, src=src):
                v = w_load[j]
                k = dst.shape[1]
                e.dma_start(dst, src[0, bass.ds(v, 1)].rearrange("o (p k) f -> (o p) k f", k=k)).then_inc(o_w.sem, 16)
            osp.steps.append(load)
        w_ok = (o_w.sem, o_w.count)
        x_got = o_in.start_indirect(opo, lambda q, tile=tile: q.indirect_dma_start(
            out=oxg, out_offset=None, in_=xn_dram,
            in_offset=bass.IndirectOffsetOnAxis(ap=idx[:, tile:tile + 1], axis=0)), end)
        pv = OVB[0].rearrange("p (k n) -> p k n", k=KD)
        for k in range(KD):
            make = lambda e, k=k: e.transpose(pv[:, k, :], oxg[:, k::KD], ident[0:CAP, 0:CAP])
            tk = ope.do(make, x_got, end)
        t = ove.do(lambda e: e.tensor_tensor(ogt, pv, bc(g2p, [P, KD, CAP]), MUL), tk)
        for k in range(KD):
            tk = ope.do(lambda e, k=k: e.matmul(OVB[1][0:CAP, :], ogt[:, k, :], w13[:, :, k, :], start=k == 0,
                                                stop=k == KD - 1), t, w_ok)
        t = oac.do(lambda e: e.activation(osg, OVB[1][0:CAP, 0:DE], ACT.Sigmoid), tk)
        t = ove.do(lambda e: e.tensor_tensor(osg, osg, OVB[1][0:CAP, 0:DE], MUL), t)
        t = ove.do(lambda e, tile=tile: e.scalar_tensor_tensor(
            osg, osg, info[:, tile, 1:2], OVB[1][0:CAP, DE:2 * DE], MUL, MUL), t)
        pv2 = OVB[0][:, 0:2 * CAP].rearrange("p (k n) -> p k n", k=2)
        for k in range(2):
            tk = ope.do(lambda e, k=k: e.transpose(pv2[:, k, :], osg[:, k::2], ident[0:CAP, 0:CAP]), t)
        t = ove.do(lambda e: e.tensor_copy(oht, pv2), tk)
        for half in range(2):
            cols = slice(half * BANK, half * BANK + BANK)
            for k in range(2):
                tk = ope.do(lambda e, half=half, k=k, cols=cols: e.matmul(
                    OVB[2 + half][0:CAP, :], oht[:, k, :], wdn[:, k, cols], start=k == 0, stop=k == 1), t)
        for half in range(2):
            cols = slice(half * BANK, half * BANK + BANK)
            t = ove.do(lambda e, half=half, cols=cols: e.tensor_copy(oxg[:, cols], OVB[2 + half][0:CAP, :]), tk)
        end = o_y.start(osp, y_dram[tile * CAP:(tile + 1) * CAP, :], oxg, t)
    over = dict(pe=ope, ve=ove, ac=oac, po=opo, sp=osp)
    for q in over.values():
        q.wait(end)

    def branch(queue, name):
        def step(e):
            v = e.value_load(ov_ids[0:1, EXTRA:EXTRA + 1], min_val=0, max_val=EXTRA)
            with e.If(v):
                over[name].play(e)
        queue.quiet(step, main_end, ov_ok)

    for q, name in zip((pe, ve, ac, po, sp), names):
        branch(q, name)

    fetch = [Arrivals(sem(f"s_fetch{i}")) for i in range(4)]
    YG = W[:, :, :].rearrange("p u (a d) -> p u a d", a=2)
    x2_out = Arrivals(sem("s_x2"))
    for i in range(NT):
        for n in range(2):
            f_ok = fetch[i].start_indirect(po, lambda q, i=i, n=n: q.indirect_dma_start(
                out=YG[:, i, n, :], out_offset=None, in_=y_dram,
                in_offset=bass.IndirectOffsetOnAxis(ap=slot_u[:, n * NT + i:n * NT + i + 1], axis=0)))
        t = tt(YG[:, i, 0, :], YG[:, i, 0, :], YG[:, i, 1, :], ADD, f_ok)
        t = tt(x1[:, i, :], x1[:, i, :], YG[:, i, 0, :], ADD, t)
        x2_stored = x2_out.start(sp, (out[0] if stop_at == 1 else x2_dram)[i * P:i * P + P, :], x1[:, i, :], t)
    x2_ok = t
    def block_two():
        m3 = [ve.last, x2_stored]
        _, h_ok, xs_rd = normalise(m_all[:, :], x2_ok, [ve.last, pe.last], g3)
        m_free = [x2_stored, ve.last, ac.last]
        t_clear = [ve.last, ac.last, pe.last]
        NAT = W[:, 0:3, :].rearrange("p a n -> p (a n)").rearrange("p (i n) -> p i n", i=NT)

        ii, jj = T[:, 0:P].bitcast(I32), T[:, P:2 * P].bitcast(I32)
        xr, sh = T[:, 2 * P:3 * P].bitcast(I32), T[:, 3 * P:4 * P].bitcast(I32)
        shf = T[:, 4 * P:5 * P]
        ti = po.do(lambda e: e.iota(ii, pattern=[[1, P]], base=0, channel_multiplier=0), t_clear)
        ti = po.do(lambda e: e.iota(jj, pattern=[[0, P]], base=0, channel_multiplier=1), t_clear)
        t = tt(xr, ii, jj, ALU.bitwise_xor, ti)
        LEVELS = 6
        level = []
        for l in range(LEVELS + 1):
            t = ts(sh, xr, l, None, ALU.arith_shift_right, None, t)
            t = cp(shf, sh, t)
            a = const(P)
            if l < LEVELS:
                t = ts(a, shf, 1.0, None, ALU.is_equal, None, t)
                t = tt(a, a, upper, MUL, t)
                level.append(a)
            else:
                same = a
                t = ts(a, shf, 0.0, None, ALU.is_equal, None, t)
        causal = const(P)
        t = tt(causal, upper, ident, ADD, t)
        t = masks_ok = tt(causal, causal, same, MUL, t)

        LEAD = TAPS - 1
        UB = T[:, 1024:1024 + 2 * (SEQ + 4)].rearrange("p (u n) -> p u n", u=2)
        SGB = T[:, 2560:2560 + 2 * SEQ].rearrange("p (u n) -> p u n", u=2)
        CV = W[:, 3, :].rearrange("p (c n) -> p c n", c=HB)
        zt = None
        for u in range(2):
            zt = ve.do(lambda e, u=u: e.memset(UB[:, u, 0:LEAD], 0.0), t_clear, zt)
        ub_free, sg_free, cv_free, cv_ok = [zt, zt], [t_clear] * 2, [t_clear] * HB, {}
        nat_ok = []

        def to_natural(blk):
            def run():
                for c in range(HB):
                    ch = blk * HB + c
                    b, ps, bf = bank()
                    for i in range(NT):
                        tk = turn(ps[:, i * P:i * P + P], CV[:, c, i * P:i * P + P], cv_ok[ch], bf,
                                  signal=i == NT - 1)
                    cv_free[c] = tk
                    bank_free[b] = act(NAT[:, :, ch * P:ch * P + P], ps.rearrange("p (i n) -> p i n", i=NT),
                                       ACT.Copy, tk, xs_rd)
                    nat_ok.append(bank_free[b])
            return run

        for blk in range(3):
            def evac(c, ps, tok):
                ch, u = blk * HB + c, c % 2
                f = act(UB[:, u, LEAD:LEAD + SEQ], ps, ACT.Copy, tok, ub_free[u])
                a = CV[:, c, :]
                t = ts(a, UB[:, u, LEAD:LEAD + SEQ], cw[:, ch, LEAD:LEAD + 1], None, MUL, None, f,
                       cv_free[c], vecs)
                for k in range(LEAD):
                    t = stt(a, UB[:, u, k:k + SEQ], cw[:, ch, k:k + 1], a, MUL, ADD, t)
                ub_free[u] = t
                g_ = act(SGB[:, u, :], a, ACT.Sigmoid, t, sg_free[u])
                cv_ok[ch] = sg_free[u] = tt(a, a, SGB[:, u, :], MUL, g_)
                return f
            product(True, hthi, htlo, KD, h_ok, evac, between=to_natural(blk - 1) if blk else None)

        ZA = m_all[:, 0:UNIT].rearrange("p (c n) -> p c n", c=HB)
        ZB = m_all[:, UNIT:2 * UNIT].rearrange("p (c n) -> p c n", c=HB)
        z_ok = []
        for n, Z in enumerate((ZA, ZB)):
            def evac(c, ps, tok):
                u = c % 2
                g_ = act(SGB[:, u, :], ps, ACT.Sigmoid, tok, sg_free[u])
                sg_free[u] = tt(Z[:, c, :], ps, SGB[:, u, :], MUL, g_, m_free)
                z_ok.append(sg_free[u])
                return sg_free[u]
            product(True, hthi, htlo, KD, h_ok, evac, between=to_natural(2) if n == 0 else None)

        NB = 2 * DH
        wba = small(KD, NB)
        ba_in = Arrivals(sem("s_ba"))
        ba_ok = ba_in.start(sp, wba, W_IN2[:, B_A:B_A + NB].rearrange("(k p) n -> p k n", p=P))
        wbah = wba_r[:, 0, :].rearrange("p (k n) -> p k n", k=KD)
        wbal = wba_r[:, 1, :].rearrange("p (k n) -> p k n", k=KD)
        t = split_act(wbah, wbal, wba, ba_ok)
        b, ps, bf = bank()
        bap = ps[:, 0:NT * NB].rearrange("p (i n) -> p i n", i=NT)
        for i in range(NT):
            for k in range(KD):
                cols = slice(i * P, i * P + P)
                tk = passes(bap[:, i, :], hthi[:, k, cols], htlo[:, k, cols], wbah[:, k, :], wbal[:, k, :],
                            k == 0, k == KD - 1, t, h_ok, bf, signal=k == KD - 1)
        ba = small(NT, NB)
        t1 = bank_free[b] = cp(ba, bap, tk)
        b, ps, bf = bank()
        mm(ps[:, 0:DH], ones[0:1, :], rows["dtb"], True, True, vecs, bf)
        tk = mm(ps[:, DH:2 * DH], ones[0:1, :], rows["alog"], True, True, signal=True)
        dta = small(2 * DH)
        t2 = bank_free[b] = cp(dta, ps[:, 0:2 * DH], tk)
        N16 = NT * DH
        beta, gl, ab, ea = small(NT, DH), small(NT, DH), small(NT, DH), small(DH)
        beta_ok = act(beta, ba[:, :, 0:DH], ACT.Sigmoid, t1)
        t = tt(gl, ba[:, :, DH:], dta[:, 0:DH].unsqueeze(1).broadcast_to([P, NT, DH]), ADD, t2)
        t = act(ab, gl, ACT.Abs, t)
        t = act(ab, ab, ACT.Exp, t, scale=-1.0)
        t = act(ab, ab, ACT.Ln, t, bias=1.0)
        te = act(ea, dta[:, DH:], ACT.Exp, t2)
        t = stt(gl, gl, 0.0, ab, MAX, ADD, t)
        t = stt(gl, gl, -1.0, ea.unsqueeze(1).broadcast_to([P, NT, DH]), MUL, MUL, t, te)
        gflat = gl.rearrange("p a b -> p (a b)")
        b, ps, bf = bank()
        mm(ps[:, 0:N16], causal, gflat, True, True, t, masks_ok, bf)
        mm(ps[:, N16:2 * N16], same, gflat, True, True, signal=True)
        for c in range(2):
            r_ = slice(64 * c, 64 * c + 64)
            tk = mm(ps[:, (2 + c) * N16:(3 + c) * N16], ones[r_, :], gflat[r_, :], True, True, pe.last,
                    signal=True)
        sums = small(4 * N16)
        t = bank_free[b] = cp(sums, ps[:, 0:4 * N16], tk)
        gc = sums[:, 0:N16]
        egc, edl, bege = small(N16), small(N16), small(N16)
        gend = small(2 * N16)
        t = tt(edl, sums[:, N16:2 * N16], gc, SUB, t)
        act(edl, edl, ACT.Exp, t)
        act(gend, sums[:, 2 * N16:], ACT.Exp, t)
        eg_ok = act(egc, gc, ACT.Exp, t)
        by_tile = lambda a, i: a[:, i * DH:(i + 1) * DH]
        betaf = beta.rearrange("p a b -> p (a b)")

        sq = W[:, 3, :].rearrange("p (i n) -> p i n", i=NT)
        tprev = [cv_free, nat_ok]
        for n in range(2):
            part = NAT[:, :, n * NH:(n + 1) * NH]
            ssn = small(N16)
            t = act(sq, part, ACT.Square, tprev)
            t = red(ssn, W[:, 3, :].rearrange("p (g d) -> p g d", d=DK), ADD, t)
            tprev = t
            r, rt = inverse_rms(ssn, N16, 1.0, t)
            if n == 0:
                rt = ts(r, r, DK ** -0.5, None, MUL, None, rt)
            for i in range(NT):
                v4 = part[:, i, :].rearrange("p (h d) -> p h d", h=DH)
                t = tt(v4, v4, bc(by_tile(r, i), [P, DH, DK]), MUL, rt, nat_ok)
        qk_ok = t

        slot_ = lambda n: (T[:, n * BANK:(n + 1) * BANK] if n < 11 else W[:, 3, (n - 11) * BANK:(n - 10) * BANK])
        heads = lambda a: a.rearrange("p (h n) -> p h n", h=DH)
        kT, kbT, qT, qdT, kd, dec, MT, TI, TT, qkT, vn, S, nwT, GR, TMP = (heads(slot_(n)) for n in range(15))
        BT, Q, u_ = kT, kbT, qT
        s_ok = ve.do(lambda e: e.memset(S, 0.0), tprev)
        clear = [ve.last, pe.last, ac.last]

        def turn4(dst, src, ready, free):
            b, ps, bf = bank()
            for h in range(DH):
                tk = turn(heads(ps)[:, h, :], src[:, h, :], ready, bf, signal=h == DH - 1)
            bank_free[b] = act(dst, heads(ps), ACT.Copy, tk, free)
            return bank_free[b], tk

        def mm4(l, r, *w):
            b, ps, bf = bank()
            for h in range(DH):
                tk = mm(heads(ps)[:, h, :], l[:, h, :], r[:, h, :], True, True, *w, bf, signal=h == DH - 1)
            return b, heads(ps), tk

        spread = lambda a, i: bc(by_tile(a, i), [P, DH, DK])
        each = lambda a: a.unsqueeze(1).broadcast_to([P, DH, P])
        o_ok = []
        for i in range(NT):
            Kn, Qn, Vn = (heads(NAT[:, i, n * NH:(n + 1) * NH]) for n in (1, 0, 2))
            kT_ok, k_rd = turn4(kT, Kn, qk_ok, clear)
            qT_ok, q_rd = turn4(qT, Qn, qk_ok, clear)
            t = kd_ok = tt(kd, Kn, spread(edl, i), MUL, eg_ok, clear, qk_ok)
            t = tt(Kn, Kn, spread(betaf, i), MUL, k_rd, beta_ok, t)
            kb_ok, kb_rd = turn4(kbT, Kn, t, clear)
            rk_ok = tt(Kn, Kn, spread(egc, i), MUL, kb_rd, eg_ok)
            bv_ok = tt(Vn, Vn, spread(betaf, i), MUL, beta_ok, nat_ok)
            t = tt(Qn, Qn, spread(egc, i), MUL, q_rd, eg_ok)
            qd_ok, _ = turn4(qdT, Qn, t, clear)
            t = tt(GR, each(causal), spread(gflat, i), MUL, clear, masks_ok)
            b, ps, bf = bank()
            tk = mm(ps, ones, GR.rearrange("p h n -> p (h n)"), True, True, t, bf, signal=True)
            t = bank_free[b] = tt(dec, heads(ps), spread(gc, i), SUB, tk, clear)
            t = ts(dec, dec, 0.0, None, MIN, None, t)
            dec_ok = act(dec, dec, ACT.Exp, t)
            b, ps, tk = mm4(kT, kbT, kT_ok, kb_ok)
            m_ok_ = bank_free[b] = tt(MT, ps, dec, MUL, tk, dec_ok, clear)
            b, ps, tk = mm4(kT, qT, kT_ok, qT_ok)
            t = bank_free[b] = tt(qkT, ps, dec, MUL, tk, dec_ok, clear)
            qk2_ok = tt(qkT, qkT, each(causal), MUL, t)
            t = tt(BT, MT, each(level[0]), MUL, tk, m_ok_)
            t = tt_ok = tt(TT, each(ident), BT, SUB, t, clear)
            ti_ok, _ = turn4(TI, TT, t, clear)
            for l in range(1, LEVELS):
                bt_ok = tt(BT, MT, each(level[l]), MUL, pe.last, tt_ok)
                b, ps, tk = mm4(BT, TI, bt_ok, ti_ok)
                q_ok2 = bank_free[b] = act(Q, ps, ACT.Copy, tk)
                if l < LEVELS - 1:
                    b, ps, tk = mm4(TT, Q, q_ok2, tt_ok)
                b2, ps2, tk2 = mm4(Q, TT, q_ok2, tt_ok)
                if l < LEVELS - 1:
                    ti_ok = bank_free[b] = tt(TI, TI, ps, SUB, tk, tk2, ti_ok)
                tt_ok = bank_free[b2] = tt(TT, TT, ps2, SUB, tk2, tt_ok)
            b, ps, tk = mm4(Kn, TT, rk_ok, tt_ok)
            nw_ok = bank_free[b] = act(nwT, ps, ACT.Copy, tk, clear, scale=-1.0)
            b, ps, tk = mm4(TT, Vn, tt_ok, bv_ok)
            u_ok2 = bank_free[b] = cp(u_, ps, tk)
            for c in range(2):
                R = slice(64 * c, 64 * c + 64)
                b, ps, tk = mm4(nwT, S, nw_ok, s_ok)
                v_ok2 = bank_free[b] = tt(vn[R], u_[R], ps[R], ADD, tk, u_ok2, clear)
                b, ps, bf = bank()
                po_ = heads(ps)
                for h in range(DH):
                    mm(po_[:, h, :], qdT[:, h, :], S[:, h, :], True, False, qd_ok, s_ok, bf)
                    tk = mm(po_[:, h, :], qkT[R, h, :], vn[R, h, :], False, True, qk2_ok, v_ok2, signal=True)
                bank_free[b] = act(Vn[R], po_[R], ACT.Copy, tk)
                o_ok.append(bank_free[b])
                b, ps, bf = bank()
                for h in range(DH):
                    tk = mm(heads(ps)[:, h, :], kd[R, h, :], vn[R, h, :], True, True, kd_ok, v_ok2, bf, signal=True)
                ge = gend[:, c * N16:(c + 1) * N16]
                t = tt(S, S, spread(ge, i), MUL, s_ok, tk, eg_ok)
                s_ok = bank_free[b] = tt(S, S, heads(ps), ADD, t)
            clear = [ve.last, pe.last, ac.last]

        O = NAT[:, :, 2 * NH:3 * NH]
        ssn = small(N16)
        sq_ = T[:, 0:UNIT]
        t = act(sq_.rearrange("p (i n) -> p i n", i=NT), O, ACT.Square, o_ok, clear)
        t = red(ssn, sq_.rearrange("p (g d) -> p g d", d=DK), ADD, t)
        r, rt = inverse_rms(ssn, N16, DK, t)
        for i in range(NT):
            v4 = heads(O[:, i, :])
            t = tt(v4, v4, bc(by_tile(r, i), [P, DH, DK]), MUL, rt, o_ok)
        tmp2 = T[:, UNIT:UNIT + 2 * BANK].rearrange("p (u n) -> p u n", u=2)
        y_ok2 = []
        for h in range(DH):
            b, ps, bf = bank()
            for i in range(NT):
                tk = turn(ps[:, i * P:i * P + P], O[:, i, h * DK:h * DK + DK], t, bf, signal=i == NT - 1)
            tq = bank_free[b] = stt(tmp2[:, h % 2, :], ps, dng, ZA[:, h, :], MUL, MUL, tk, vecs, z_ok, y_ok2[-2:])
            y_ok2.append(split_act(yhi[:, h, :], ylo[:, h, :], tmp2[:, h % 2, :], tq))
        nat_free2 = [tk, y_ok2[-1]]

        vt = natural_block(W[:, 0, :], W[:, 3, :], nat_free2, nat_free2)
        n_ok = group_norm(W[:, 0, :], W[:, 3, :], SBD, vt)
        q_ok, rd = turn_block(W[:, 0, :], W[:, 1, :], gq8["q2"], n_ok, nat_free2)
        vt = natural_block(W[:, 0, :], W[:, 3, :], [rd, n_ok], [n_ok])
        n_ok = group_norm(W[:, 0, :], W[:, 3, :], SBD, vt)
        k_ok, rd = turn_block(W[:, 0, :], W[:, 2, :], halves["k2"], n_ok, nat_free2)
        v_ok = natural_block(W[:, 0, :], None, [rd, n_ok])
        qS = W[:, 1, :].rearrange("p (c n) -> p c n", c=HB)
        kS = W[:, 2, :].rearrange("p (c n) -> p c n", c=HB)
        vS = W[:, 0, :].rearrange("p (i n) -> p i n", i=NT)
        tri, nones, negm = level[0], level[1], level[2]
        t = tt(tri, upper, ones, SUB, pe.last, ve.last)
        t = ts(negm, tri, -NEG, None, MUL, None, t)
        tri_ok = ts(nones, ones, -1.0, None, MUL, None, t)
        widths = [SEQ - P * j for j in range(NT)]
        offs = [sum(widths[:j]) for j in range(NT)]
        SPW = sum(widths)
        SP_ = T[:, 0:2 * SPW].rearrange("p (u n) -> p u n", u=2)
        A_ = T[:, 2 * SPW:4 * SPW].rearrange("p (u n) -> p u n", u=2)
        L_ = W[:, 3, :].rearrange("p (u n) -> p u n", u=4)
        sp_free, a_free, l_free = [[y_ok2, ve.last]] * 2, [[y_ok2, ve.last]] * 2, [n_ok] * 4
        on2 = W[:, 3, 0:BANK]
        OUT_ = T[:, 4 * SPW:4 * SPW + BANK]
        out_free = y_ok2
        yb2 = []
        li = 0
        for h in range(SBH):
            u, pair, R = h % 2, h // 2, slice(64 * (h % 2), 64 * (h % 2) + 64)
            held, sp_ok = [bank() for _ in range(NT)], []
            for j in range(NT):
                w = widths[j]
                tk = mm(held[j][1][:, 0:w], kS[R, pair, j * P:j * P + P], qS[R, pair, j * P:SEQ], True, True,
                        q_ok, k_ok, held[j][2], signal=True, part=True)
                l = L_[:, li % 4, 0:w]
                t = act(l, held[j][1][:, 0:w], ACT.Abs, tk, l_free[li % 4])
                t = act(l, l, ACT.Exp, t, scale=-1.0)
                t = act(l, l, ACT.Ln, t, bias=1.0)
                s_ = SP_[:, u, offs[j]:offs[j] + w]
                t = stt(s_, held[j][1][:, 0:w], 0.0, l, MAX, ADD, t, sp_free[u])
                l_free[li % 4] = t
                li += 1
                sp_ok.append(tt(s_[:, 0:P], s_[:, 0:P], upper, MUL, t))
            a_ok = []
            for j in range(NT):
                ps = held[j][1]
                mm(ps[:, 0:P], ident, negm, False, False, sp_ok[j], tri_ok, part=True)
                for j2 in range(j, NT):
                    tk = mm(ps[:, (j2 - j) * P:widths[j]], tri if j2 == j else nones,
                            SP_[:, u, offs[j2]:offs[j2] + widths[j2]], False, j2 == NT - 1, sp_ok[j2],
                            signal=j2 == NT - 1, part=True)
                t = bank_free[held[j][0]] = act(A_[:, u, offs[j]:offs[j] + widths[j]], ps[:, 0:widths[j]], ACT.Exp,
                                                tk, a_free[u])
                a_ok.append(t)
            sp_free[u] = tk
            if h % 2 == 0:
                ob, ops, obf = bank()
                o3 = ops.rearrange("p (i n) -> p i n", i=NT)
            for i in range(NT):
                for j in range(i + 1):
                    lo_ = offs[j] + (i - j) * P
                    tk = mm(o3[:, i, 64 * (h % 2):64 * (h % 2) + 64], A_[:, u, lo_:lo_ + P],
                            vS[:, j, h * SBD:(h + 1) * SBD], j == 0, j == i, a_ok, v_ok, obf, signal=i == NT - 1)
            a_free[u] = tk
            if h % 2:
                t = bank_free[ob] = act(OUT_, ops, ACT.Copy, tk, out_free)
                b, ps, bf = bank()
                for i in range(NT):
                    tk = turn(ps[:, i * P:i * P + P], OUT_[:, i * P:i * P + P], t, bf, signal=i == NT - 1)
                t = bank_free[b] = tt(OUT_, ps, ZB[:, pair, :], MUL, tk, z_ok)
                out_free = split_act(yhi[:, 4 + pair, :], ylo[:, 4 + pair, :], OUT_, t)
                yb2.append(out_free)

        fr = [pe.last, ve.last]
        g, g_ok = gates(bg2, 0, fr)
        m_ok2 = merge_first(yhi[:, 0:4, :], ylo[:, 0:4, :], HB, y_ok2, g, g_ok, fr)
        g, g_ok = gates(bg2, KD, [pe.last, m_ok2])
        parts = merge_second(yhi[:, 4:8, :], ylo[:, 4:8, :], HB, yb2, g, g_ok, fr)
        x_ok = x_in.start(sp, xw, x2_dram.rearrange("(i p) d -> p i d", p=P), fr, x2_stored)
        o_st = Arrivals(sem("s_out"))
        for b in range(2):
            def evac(c, ps, tok):
                cols = slice(b * BANK, b * BANK + BANK)
                t = tt(xw[:, c, cols], ps, xw[:, c, cols], ADD, tok, x_ok)
                end = o_st.start(sp, out[0, c * P:c * P + P, cols], xw[:, c, cols], t)
                return t
            product(False, hthi, htlo, KD, parts, evac)
        sp.wait((o_st.sem, o_st.count))

    if stop_at != 1:
        block_two()
    sp.wait(x2_stored)

    with nc.Block() as block:
        @block.sync
        def _(e):
            sp.play(e)

        @block.tensor
        def _(e):
            pe.play(e)

        @block.vector
        def _(e):
            ve.play(e)

        @block.scalar
        def _(e):
            ac.play(e)

        @block.gpsimd
        def _(e):
            po.play(e)
    ctx.close()


INPUTS = ("x", "norm1_g", "w_in", "v_norm_g", "w_s", "b_s", "q_norm_g", "k_norm_g", "lambda_q1",
          "lambda_k1", "lambda_q2", "lambda_k2", "sub_norm_g", "w_up_a", "w_up_b", "w_gate", "b_gate",
          "w_out", "norm2_g", "w_rg", "b_rg", "w_re", "b_re", "w1", "w3", "w2", "norm_gain_2",
          "w_in_2", "b_gate_2", "conv_w_2", "a_log_2", "dt_bias_2", "dn_out_gain_2",
          "sb_q_gain_2", "sb_k_gain_2", "w_up_a_2", "w_up_b_2", "w_out_2")


def kernel(**inputs):
    import numpy as np
    from concourse import bacc
    from concourse.bass_utils import run_bass_kernel_spmd

    nc = bacc.Bacc("TRN2", target_bir_lowering=False, num_devices=1)
    arrays, args = {}, []
    for name in INPUTS:
        a = np.ascontiguousarray(inputs[name])
        arrays[f"in_{name}"] = a
        args.append(nc.dram_tensor(f"in_{name}", a.shape, mybir.dt.from_np(a.dtype),
                                   kind="ExternalInput").ap())
    shape = inputs["x"].shape
    args.append(nc.dram_tensor("result", shape, F32, kind="ExternalOutput").ap())
    build(nc, *args)
    r = run_bass_kernel_spmd(nc, [arrays], core_ids=[0])
    return r.results[0]["result"]
```

```python
from contextlib import ExitStack

import concourse.bass as bass
import concourse.mybir as mybir

F32 = mybir.dt.float32
F32R = mybir.dt.float32r
I32 = mybir.dt.int32
U32 = mybir.dt.uint32
ALU = mybir.AluOpType
ACT = mybir.ActivationFunctionType
AX_X = mybir.AxisListType.X

P = 128
BANKS = 8
BANK = 512
EPS = 1e-6
NEG = -1.0e30


class Queue:

    def __init__(self, sem):
        self.sem, self.count, self.steps, self.seen, self.last = sem, 0, [], {}, None

    def wait(self, *waits):
        for w in waits:
            if isinstance(w, list):
                self.wait(*w)
            elif w is not None and self.seen.get(w[0].name, 0) < w[1]:
                self.seen[w[0].name] = w[1]
                self.steps.append(lambda e, w=w: e.wait_ge(w[0], w[1]))

    def quiet(self, make, *waits):
        self.wait(*waits)
        self.steps.append(make)

    def do(self, make, *waits):
        self.wait(*waits)
        self.count += 1
        self.steps.append(lambda e: make(e).then_inc(self.sem, 1))
        self.last = (self.sem, self.count)
        return self.last

    def play(self, engine):
        for step in self.steps:
            step(engine)


class Arrivals:

    def __init__(self, sem):
        self.sem, self.count = sem, 0

    def start(self, queue, out, in_, *waits):
        queue.wait(*waits)
        self.count += 16
        queue.steps.append(lambda e: e.dma_start(out, in_).then_inc(self.sem, 16))
        return (self.sem, self.count)

    def start_indirect(self, queue, make, *waits):
        queue.wait(*waits)
        self.count += 16
        queue.steps.append(lambda e: make(e).then_inc(self.sem, 16))
        return (self.sem, self.count)


def build(nc, x, norm1_g, w_in, v_norm_g, w_s, b_s, q_norm_g, k_norm_g, lambda_q1, lambda_k1,
          lambda_q2, lambda_k2, sub_norm_g, w_up_a, w_up_b, w_gate, b_gate, w_out, norm2_g, w_rg,
          b_rg, w_re, b_re, w1, w3, w2, norm_gain_2, w_in_2, b_gate_2, conv_w_2, a_log_2,
          dt_bias_2, dn_out_gain_2, sb_q_gain_2, sb_k_gain_2, w_up_a_2, w_up_b_2, w_out_2, out):
    ctx = ExitStack()
    sem = lambda name: ctx.enter_context(nc.semaphore(name))
    sb = lambda name, shape, dt=F32: ctx.enter_context(nc.sbuf_tensor(name, shape, dt))

    SEQ, D = x.shape[1], x.shape[2]
    NT = SEQ // P
    KD = D // P
    HB = 4
    UNIT = 2048
    G_A, DG = v_norm_g.shape[1], v_norm_g.shape[2]
    HEADS1, HD = 8, q_norm_g.shape[1]
    DV1 = 2 * HD
    LAM_INIT = 0.8 - 0.6 * 1.0
    NG, NE = w_rg.shape[2], w_re.shape[2]
    EPG = NE // NG
    DE = w1.shape[3]
    TOPK = 2
    CAP = 64
    EXTRA = (SEQ * TOPK) // (CAP + 1)
    SLOTS = (NE + EXTRA) * CAP
    DH, DK = a_log_2.shape[1], 128
    SBH, SBD = 8, sb_q_gain_2.shape[1]
    TAPS = conv_w_2.shape[1]
    CHUNK2 = 64

    xn_dram = nc.dram_tensor("xn_scratch", [SEQ, D], F32, kind="Internal").ap()
    y_dram = nc.dram_tensor("y_scratch", [SLOTS, D], F32, kind="Internal").ap()
    gate_dram = nc.dram_tensor("gate_scratch", [KD, P, SEQ], F32, kind="Internal").ap()
    x2_dram = nc.dram_tensor("x2_scratch", [SEQ, D], F32, kind="Internal").ap()

    NR, NS = 3, 2
    raw = sb("raw", [P, NR, UNIT])
    whi = sb("whi", [P, NS, UNIT], F32R)
    wlo = sb("wlo", [P, NS, UNIT], F32R)
    hthi = sb("hthi", [P, KD, SEQ], F32R)
    htlo = sb("htlo", [P, KD, SEQ], F32R)
    yhi = sb("yhi", [P, KD, SEQ], F32R)
    ylo = sb("ylo", [P, KD, SEQ], F32R)
    m_all = sb("merged", [P, KD * SEQ])
    W = sb("work", [P, 4, UNIT])
    T = sb("scratch", [P, 5632])
    C = sb("consts", [P, 1536])
    SM = sb("smalls", [P, 2360])
    SI = sb("small_ints", [P, 128], I32)
    wba_r = sb("wba_r", [P, 2, KD * 2 * DH], F32R)
    PS = ctx.enter_context(nc.psum_tensor("PS", [P, BANKS, BANK], F32))

    pe, ve, ac, po, sp = (Queue(sem(n)) for n in ("s_pe", "s_ve", "s_ac", "s_po", "s_sp"))

    def mm(o, l, r, start, stop, *w, signal=False, part=False):
        make = lambda e: e.matmul(o, l, r, start=start, stop=stop, skip_group_check=part)
        return pe.do(make, *w) if signal else pe.quiet(make, *w)

    def turn(o, i, *w, signal=False):
        n = i.shape[0]
        make = lambda e: e.transpose(o, i, ident[0:n, 0:n])
        return pe.do(make, *w) if signal else pe.quiet(make, *w)

    table = [None]

    def act(o, i, f, *w, bias=0.0, scale=1.0, acc=None):
        need = {ACT.Exp: "natural_log_exp_and_others", ACT.Ln: "natural_log_exp_and_others",
                ACT.Sigmoid: "sigmoid_and_others"}.get(f)
        if need and need != table[0]:
            table[0] = need
            ac.quiet(lambda e: e.preload_act_table_set(need))
        if acc is None:
            return ac.do(lambda e: e.activation(o, i, f, bias=bias, scale=scale), *w)
        return ac.do(lambda e: e.activation(o, i, f, bias=bias, scale=scale, accum_out=acc), *w)

    def tt(o, a, b, op, *w, q=None):
        return (q or ve).do(lambda e: e.tensor_tensor(o, a, b, op), *w)

    def ts(o, a, s1, s2, op0, op1, *w):
        if s2 is None:
            return ve.do(lambda e: e.tensor_scalar(o, a, s1, None, op0), *w)
        return ve.do(lambda e: e.tensor_scalar(o, a, s1, s2, op0, op1), *w)

    def stt(o, a, s, b, op0, op1, *w):
        return ve.do(lambda e: e.scalar_tensor_tensor(o, a, s, b, op0, op1), *w)

    def cp(o, a, *w):
        return ve.do(lambda e: e.tensor_copy(o, a), *w)

    def red(o, a, op, *w, neg=False):
        return ve.do(lambda e: e.tensor_reduce(o, a, AX_X, op, negate=neg), *w)

    MUL, ADD, SUB, MAX, MIN = ALU.mult, ALU.add, ALU.subtract, ALU.max, ALU.min

    def bc(ap, shape):
        return ap.unsqueeze(len(ap.shape)).broadcast_to(shape)

    def as_f32(ap):
        return ap.bitcast(F32)

    bank_free = [None] * BANKS
    bank_at = [0]

    def bank():
        while bank_free[bank_at[0] % BANKS] == "held":
            bank_at[0] += 1
        b = bank_at[0] % BANKS
        bank_at[0] += 1
        free, bank_free[b] = bank_free[b], "held"
        return b, PS[:, b, :], free

    sm_at = [0]

    def small(*shape):
        n = 1
        for s in shape:
            n *= s
        a = SM[:, sm_at[0]:sm_at[0] + n]
        sm_at[0] += n
        assert sm_at[0] <= 2360, sm_at
        return a if len(shape) == 1 else a.rearrange(
            "p (a b) -> p a b", b=shape[1]) if len(shape) == 2 else a.rearrange(
            "p (a b c) -> p a b c", b=shape[1], c=shape[2])

    c_at = [0]

    def const(n):
        a = C[:, c_at[0]:c_at[0] + n]
        c_at[0] += n
        assert c_at[0] <= 1536
        return a

    ident, ones, upper = const(P), const(P), const(P)
    t = po.do(lambda e: e.memset(ident, 0.0))
    t = po.do(lambda e: e.affine_select(out=ident, in_=ident, compare_op=ALU.not_equal, fill=1.0,
                                        base=0, pattern=[[-1, P]], channel_multiplier=1), t)
    ident_ok = t
    t = po.do(lambda e: e.memset(ones, 1.0))
    ones_ok = t
    t = po.do(lambda e: e.affine_select(out=upper, in_=ones, compare_op=ALU.is_gt, fill=0.0,
                                        base=0, pattern=[[1, P]], channel_multiplier=-1), t)
    const_ok = t

    x_in = Arrivals(sem("s_x"))
    xv = x.rearrange("b (i p) d -> p (b i) d", p=P)
    x_tiles = [Arrivals(sem(f"s_xtile{i}")) for i in range(NT)]
    x_ok = [x_tiles[i].start(sp, m_all[:, i * D:(i + 1) * D], xv[:, i, :]) for i in range(NT)]

    vec_in = Arrivals(sem("s_vec"))
    vrows = sb("vector_rows", [P, P])
    vcols = const(P)
    v_at, vec_tok = [0], [None]
    vr_ok = ve.do(lambda e: e.memset(vrows[:, :], 0.0))

    def columns(ap, n):
        at = v_at[0]
        vec_tok[0] = vec_in.start(sp, vrows[at:at + n, :], ap, vr_ok)
        v_at[0] += n
        return vcols[:, at:at + n]

    g1 = columns(norm1_g[0].rearrange("(k p) -> k p", p=P), KD)
    gv = columns(v_norm_g[0], G_A)
    bg = columns(b_gate[0].rearrange("(k p) -> k p", p=P), 2 * KD)
    g2 = columns(norm2_g[0].rearrange("(k p) -> k p", p=P), KD)
    g3 = columns(norm_gain_2[0].rearrange("(k p) -> k p", p=P), KD)
    bg2 = columns(b_gate_2[0].rearrange("(k p) -> k p", p=P), 2 * KD)
    sg = columns(sub_norm_g, 1)
    dng = columns(dn_out_gain_2, 1)
    cw = columns(conv_w_2[0].rearrange("k (c p) -> (k c) p", p=P), 12 * TAPS).rearrange(
        "p (k c) -> p c k", k=TAPS)
    halves = {}
    for name, g in (("q1", q_norm_g), ("k1", k_norm_g), ("q2", sb_q_gain_2), ("k2", sb_k_gain_2)):
        at = v_at[0]
        for half in range(2):
            vec_tok[0] = vec_in.start(sp, vrows[at:at + 1, 64 * half:64 * half + 64], g, vr_ok)
        halves[name] = vcols[:, at:at + 1]
        v_at[0] += 1
    assert v_at[0] <= P
    g2p = small(KD)
    vec_tok[0] = vec_in.start(sp, g2p, norm2_g[0].rearrange("(p k) -> p k", k=KD))
    rows = {}

    def row(name, ap, n):
        a = small(n)[0:1, :]
        vec_tok[0] = vec_in.start(sp, a, ap)
        rows[name] = a

    for name, v in (("lq1", lambda_q1), ("lk1", lambda_k1), ("lq2", lambda_q2), ("lk2", lambda_k2)):
        row(name, v, HD)
    router_bias = small(NG + NE)[0:1, :]
    vec_in.start(sp, router_bias[:, 0:NG], b_rg)
    vec_in.start(sp, router_bias[:, NG:], b_re)
    row("alog", a_log_2, DH)
    row("dtb", dt_bias_2, DH)
    b, ps, bf = bank()
    tk = pe.do(lambda e: e.transpose(PS[:, 0, 0:P], vrows[:, :], ident), vec_tok[0], ident_ok)
    bank_free[b] = vecs = [cp(vcols, ps[:, 0:P], tk), vec_tok[0]]

    units = []

    def matrix(src, rows_, c0):
        for r in range(rows_ // BANK):
            units.append([(lambda a: a.rearrange("p (k n) -> p k n", k=HB),
                           src[r * BANK:(r + 1) * BANK, c0:c0 + BANK].rearrange("(k p) n -> p k n", p=P))])

    W_IN, W_G, A_W = w_in[0], w_gate[0], D
    for b in range(2):
        matrix(W_IN, D, A_W + BANK * b)
        matrix(W_IN, D, BANK * b)
    for b in range(2):
        matrix(W_G, D, BANK * b)
    for b in range(2):
        matrix(w_up_a[0], D, BANK * b)
    for b in range(2):
        for base in (2 * D, 3 * D, 4 * D):
            matrix(W_IN, D, base + BANK * b)
        matrix(W_G, D, D + BANK * b)
    for b in range(2):
        matrix(w_up_b[0], D, BANK * b)
    for b in range(2):
        matrix(w_out[0], D, BANK * b)

    def expert_up(e):
        for kh in range(2):
            units.append([
                (lambda a, j=j: a.rearrange("p (j k f) -> p j k f", j=2, k=HB)[:, j],
                 w[0, e].rearrange("(p k) f -> p k f", k=KD)[:, HB * kh:HB * kh + HB, :])
                for j, w in enumerate((w1, w3))])

    def expert_down(e):
        units.append([(lambda a: a.rearrange("p (k n) -> p k n", k=2),
                       w2[0, e].rearrange("(p k) n -> p k n", k=2))])

    for e in range(NE + 1):
        if e < NE:
            expert_up(e)
        if e:
            expert_down(e - 1)
    after_experts = len(units)
    W_IN2 = w_in_2[0]
    NH = DH * DK
    Z_A, B_A = 3 * NH, 4 * NH
    QKV_B = B_A + 2 * DH
    Z_B = QKV_B + 3 * SBH * SBD
    G_2 = Z_B + SBH * SBD
    for b in range(3):
        matrix(W_IN2, D, BANK * b)
    matrix(W_IN2, D, Z_A)
    matrix(W_IN2, D, Z_B)
    for b in range(3):
        matrix(W_IN2, D, QKV_B + BANK * b)
    for b in range(2):
        matrix(W_IN2, D, G_2 + BANK * b)
    for b in range(2):
        matrix(w_up_a_2[0], NH, BANK * b)
    for b in range(2):
        matrix(W_IN2, D, G_2 + D + BANK * b)
    for b in range(2):
        matrix(w_up_b_2[0], SBH * SBD, BANK * b)
    for b in range(2):
        matrix(w_out_2[0], D, BANK * b)

    NB = 2 * DH
    wba = small(KD, NB)
    ba_in = Arrivals(sem("s_ba"))
    ba_ok = ba_in.start(sp, wba, W_IN2[:, B_A:B_A + NB].rearrange("(k p) n -> p k n", p=P))

    LENT_RAW, LENT_SPLIT = 2, 3
    raw_in = [Arrivals(sem(f"s_raw{i}")) for i in range(NR + LENT_RAW)]
    raw_slots = [(s, None) for s in range(NR)]
    raw_slot = {}
    slots = [(s, None) for s in range(NS)]
    split_slot, split_parts = {}, {}
    split_ok = {}
    loaded, split = [0], [0]
    load_limit = [len(units)]
    raw_tok = {}

    def place_of(s):
        if s < NS:
            return whi[:, s, :], wlo[:, s, :]
        if s == NS + 2:
            return tuple(a[:, HB:2 * HB, :].rearrange("p k n -> p (k n)") for a in (yhi, ylo))
        at = slice(HB * (s - NS), HB * (s - NS) + HB)
        return tuple(a[:, at, :].rearrange("p k n -> p (k n)") for a in (hthi, htlo))

    def raw_place(s):
        return raw[:, s, :] if s < NR else T[:, BANK + UNIT * (s - NR):BANK + UNIT * (s - NR + 1)]

    def free_of(places, own, j):
        for a in places:
            if a[0] < own or j < after_experts:
                places.remove(a)
                return a
        return None, None

    def load_more(upto):
        while loaded[0] < min(upto, load_limit[0]):
            j = loaded[0]
            s, free = free_of(raw_slots, NR, j)
            if s is None:
                break
            raw_slot[j] = s
            for place, src in units[j]:
                raw_tok[j] = raw_in[s].start(sp, place(raw_place(s)), src, free)
            loaded[0] += 1

    def split_more(upto):
        while split[0] < min(upto, len(units)):
            j = split[0]
            load_more(j + 1)
            if j not in raw_slot:
                break
            s, free = free_of(slots, NS, j)
            if s is None:
                break
            split_slot[j] = s
            hs, ls = split_parts[j] = place_of(s)
            r = raw_place(raw_slot[j])
            hi = act(hs, r, ACT.Copy, raw_tok[j], free)
            lo = tt(ls, r, as_f32(hs), SUB, raw_tok[j], free, hi)
            split_ok[j] = [hi, lo]
            raw_slots.append((raw_slot[j], [hi, lo]))
            split[0] += 1
            load_more(len(units))

    unit_at = [0]

    def take():
        j = unit_at[0]
        unit_at[0] += 1
        split_more(j + 1)
        assert split[0] > j, "no free slot for a split unit"
        return j, *split_parts[j], split_ok[j]

    def done(j, tok, more=True):
        slots.append((split_slot[j], tok))
        if more:
            split_more(split[0] + len(slots))

    load_more(NR)

    def passes(o, lh, ll, rh, rl, start, stop, *w, signal=False):
        mm(o, lh, rh, start, False, *w)
        mm(o, lh, rl, False, False)
        return mm(o, ll, rh, False, stop, signal=signal)

    def product(turned, hi, lo, kt, ready, evac, between=None, by_k=None, early=None):
        held = [bank() for _ in range(HB)]
        tok = [None] * HB
        for kh in range(kt // HB):
            j, wh, wl, ok = take()
            wh, wl = (a.rearrange("p (k n) -> p k n", k=HB) for a in (wh, wl))
            for c in range(HB):
                cols = slice(c * P, c * P + P)
                for k in range(HB):
                    kk = kh * HB + k
                    if turned:
                        l, r = (wh[:, k, cols], wl[:, k, cols]), (hi[:, kk, :], lo[:, kk, :])
                    else:
                        l, r = (hi[:, kk, cols], lo[:, kk, cols]), (wh[:, k, :], wl[:, k, :])
                    last = kk == kt - 1
                    w = [ok, ready, held[c][2]] if k == 0 else []
                    if by_k:
                        w.append(by_k[kk])
                    end = passes(held[c][1], *l, *r, kk == 0, last, *w, signal=k == HB - 1)
                tok[c] = end
            if early and kh == 0:
                early()
            done(j, end)
        if between:
            between()
        for c in range(HB):
            bank_free[held[c][0]] = evac(c, held[c][1], tok[c])

    def product_steps(hi, lo, kt, ready, evac):
        parts = []
        for kh in range(kt // HB):
            j, wh, wl, ok = take()
            parts.append((j, ok, *(a.rearrange("p (k n) -> p k n", k=HB) for a in (wh, wl))))
        for c in range(HB):
            cols = slice(c * P, c * P + P)
            b, ps, bf = bank()
            for kk in range(kt):
                j, ok, wh, wl = parts[kk // HB]
                tk = passes(ps, wh[:, kk % HB, cols], wl[:, kk % HB, cols], hi[:, kk, :], lo[:, kk, :],
                            kk == 0, kk == kt - 1, ok, ready, bf, signal=kk == kt - 1)
                if kk < kt - 1:
                    yield
            bank_free[b] = evac(c, ps, tk)
            yield
        for j, *_ in parts:
            done(j, tk)

    rms_tmp = small(4 * 32)

    def inverse_rms(ss, n, count, ready, eps=EPS):
        v, l, y, h = (rms_tmp[:, i * 32:i * 32 + n] for i in range(4))
        r = small(n)
        return inverse_rms_in(v, l, y, h, r, ss, count, ready, eps)

    def inverse_rms_in(v, l, y, h, r, ss, count, ready, eps=EPS):
        tv = ts(v, ss, 1.0 / count, eps, MUL, ADD, ready)
        tl = act(l, v, ACT.Ln, tv)
        ty = act(y, l, ACT.Exp, tl, scale=-0.5)
        t = stt(h, y, -0.5, y, MUL, MUL, ty)
        t = tt(h, h, v, MUL, t)
        return r, stt(r, h, 1.5, y, ADD, MUL, t)

    def normalise(src, ready, free, gains, keep=None, between=None, each=None):
        ss = small(NT)
        xs = W[:, 0:2, :].rearrange("p a n -> p (a n)").rearrange("p (i d) -> p i d", i=NT)
        s = src.rearrange("p (i d) -> p i d", i=NT)
        for i in range(NT):
            t = act(xs[:, i, :], s[:, i, :], ACT.Square, ready[i] if len(ready) == NT else ready, free,
                    acc=ss[:, i:i + 1])
        r, rt = inverse_rms(ss, NT, D, t)
        toks = [ts(xs[:, i, :], s[:, i, :], r[:, i:i + 1], None, MUL, None, rt, t) for i in range(NT)]
        if between:
            between()
        for k in range(KD):
            b, ps, bf = bank()
            for i in range(NT):
                tk = turn(ps[:, i * P:i * P + P], xs[:, i, k * P:k * P + P], toks, bf, ident_ok,
                          signal=i == NT - 1)
            if keep is not None:
                bank_free[b] = ts(keep[:, k, :], ps, gains[:, k:k + 1], None, MUL, None, tk, vecs, ready)
                t2 = bank_free[b]
                if each:
                    if k:
                        each(k - 1, kept)
                    kept = t2
                    if k == KD - 1:
                        each(k, kept)
                continue
            h = act(hthi[:, k, :], ps, ACT.Copy, tk, vecs, free, scale=gains[:, k:k + 1])
            t2 = bank_free[b] = stt(htlo[:, k, :], ps, gains[:, k:k + 1], as_f32(hthi[:, k, :]),
                                    MUL, SUB, h)
        return toks, t2, tk

    def split_act(hi_o, lo_o, src, *w):
        h = act(hi_o, src, ACT.Copy, *w)
        return tt(lo_o, src, as_f32(hi_o), SUB, h)

    wbah = wba_r[:, 0, :].rearrange("p (k n) -> p k n", k=KD)
    wbal = wba_r[:, 1, :].rearrange("p (k n) -> p k n", k=KD)

    _, ht_ok, _ = normalise(m_all[:, :], x_ok, None, g1, between=lambda: split_more(1))
    split_more(NS)
    x_read = ve.last

    wba_ok = split_act(wbah, wbal, wba, ba_ok)

    ws_in = Arrivals(sem("s_ws"))
    wsn = W[:, 3, 0:1024].rearrange("p (g s) -> p g s", g=G_A)
    wst = T[:, 0:1024].rearrange("p (g s) -> p g s", g=G_A)
    bsb = T[:, 1024:2048]
    bsrow = T[0:1, 2048:3072]
    ws_in.start(sp, wsn, w_s[0].rearrange("g t s -> t g s"))
    ws_ok = ws_in.start(sp, bsrow, b_s[0:1].rearrange("o g t -> o (g t)"))
    t_ws = po.do(lambda e: e.affine_select(out=wsn, in_=wsn, compare_op=ALU.is_ge, fill=0.0, base=0,
                                        pattern=[[0, G_A], [-1, P]], channel_multiplier=1), ws_ok)
    zrows = T[0:EXTRA * CAP // 8, 4608:4608 + D]
    t = po.do(lambda e: e.memset(zrows, 0.0))
    yz = Arrivals(sem("s_yzero"))
    for n in range(8):
        yz_ok = yz.start(po, y_dram[NE * CAP:, :].rearrange("(n p) d -> n p d", n=8)[n], zrows, t)

    def group_norm(dst, squares, width, ready):
        n = UNIT // width
        ss = small(n)
        ts_ = red(ss, squares.rearrange("p (g d) -> p g d", d=width), ADD, ready)
        r, rt = inverse_rms(ss, n, width, ts_)
        d = dst.rearrange("p (g d) -> p g d", d=width)
        return tt(d, d, bc(r, [P, n, width]), MUL, rt)

    def natural_block(dst, squares, free, sq_free=None, between=None, early=None):
        toks = []

        def evac(c, ps, tok):
            o = dst.rearrange("p (i n) -> p i n", i=NT)[:, c, :]
            if squares is None:
                toks.append(act(o, ps, ACT.Copy, tok, free))
                return toks[-1]
            a = act(o, ps, ACT.Copy, tok, free)
            toks.append(act(squares.rearrange("p (i n) -> p i n", i=NT)[:, c, :], o, ACT.Square, a, sq_free))
            return a
        product(False, hthi, htlo, KD, ht_ok, evac, between, early=early)
        return toks

    def spatial_constants(t):
        for half in range(2):
            b, ps, bf = bank()
            for g in range(4):
                tk = turn(ps[:, g * P:g * P + P], wsn[:, half * 4 + g, :], t, bf, signal=g == 3)
            bank_free[b] = wst_ok = cp(wst[:, half * 4:half * 4 + 4, :], ps.rearrange("p (g s) -> p g s", g=4), tk)
            b, ps, bf = bank()
            tk = mm(ps, ones[0:1, :], bsrow[:, half * BANK:half * BANK + BANK], True, True, ws_ok,
                    ones_ok, bf, signal=True)
            bank_free[b] = bsb_ok = cp(bsb[:, half * BANK:half * BANK + BANK], ps, tk)
        return wst_ok, bsb_ok

    w_free = [[pe.last, ve.last]] * 4
    y_ok = []
    spat_tmp = T[:, 3072:3072 + 2 * BANK].rearrange("p (a n) -> p a n", a=2)
    for b in range(2):
        vt = natural_block(W[:, 0, :], W[:, 2, :], w_free[0], w_free[2])
        if b == 0:
            wst_ok, bsb_ok = spatial_constants(t_ws)
        vn_ok = group_norm(W[:, 0, :], W[:, 2, :], DG, vt)
        ut = W[:, 1, :].rearrange("p (c n) -> p c n", c=HB)
        u_ok = {}

        def evac_u(c, ps, tok):
            u_ok[c] = act(ut[:, c, :], ps, ACT.Copy, tok, w_free[1])
            return u_ok[c]
        product(True, hthi, htlo, KD, ht_ok, evac_u)
        vn = W[:, 0, :].rearrange("p (i n) -> p i n", i=NT)
        for g in range(4):
            gg = b * 4 + g
            bb, ps, bf = bank()
            for i in range(NT):
                tk = mm(ps[:, i * P:i * P + P], vn[:, i, g * P:g * P + P], wst[:, gg, :], True, True,
                        vn_ok, wst_ok, bf, signal=i == NT - 1)
            tmp = spat_tmp[:, g % 2, :]
            t = stt(tmp.rearrange("p (i s) -> p i s", i=NT), ps.rearrange("p (i s) -> p i s", i=NT),
                    gv[:, gg:gg + 1], bsb[:, gg * P:gg * P + P].unsqueeze(1).broadcast_to([P, NT, P]),
                    MUL, ADD, tk, bsb_ok, vecs, y_ok[-2:])
            bank_free[bb] = t
            t = tt(tmp, tmp, ut[:, g, :], MUL, t, u_ok[g])
            u_read = t
            y_ok.append(split_act(yhi[:, gg, :], ylo[:, gg, :], tmp, t))
        w_free = [tk, u_read, vn_ok, None]

    mg = m_all[:, :].rearrange("p (k n) -> p k n", k=KD)

    def gates(bias, c0, free):
        g = W[:, 0:2, :].rearrange("p a n -> p (a n)").rearrange("p (k n) -> p k n", k=KD)
        ok = []
        for b in range(2):
            def evac(c, ps, tok):
                k = b * HB + c
                ok.append(act(g[:, k, :], ps, ACT.Sigmoid, tok, free, vecs, bias=bias[:, c0 + k:c0 + k + 1]))
                return ok[-1]
            product(True, hthi, htlo, KD, ht_ok, evac)
        return g, ok

    def merge_first(hi, lo, kt, ready, g, g_ok, free):
        for b in range(2):
            def evac(c, ps, tok):
                k = b * HB + c
                return tt(mg[:, k, :], ps, g[:, k, :], MUL, tok, g_ok, free)
            product(True, hi, lo, kt, None, evac, by_k=ready)
        return ve.last

    merge_tmp = T[:, 4608:4608 + 2 * BANK].rearrange("p (a n) -> p a n", a=2)

    def merge_second(hi, lo, kt, ready, g, g_ok, free):
        ok, adds, pending = [], [], []
        h_free = pe.last

        def low_part():
            k, h = pending.pop(0)
            ok.append(tt(htlo[:, k, :], mg[:, k, :], as_f32(hthi[:, k, :]), SUB, h))

        for b in range(2):
            def evac(c, ps, tok):
                k = b * HB + c
                tmp = merge_tmp[:, k % 2, :]
                f = tt(tmp, ps, g[:, k, :], MUL, tok, g_ok, free, adds[-2:])
                adds.append((ve.sem, ve.count + 1))
                t = tt(mg[:, k, :], mg[:, k, :], tmp, ADD, f)
                h = act(hthi[:, k, :], mg[:, k, :], ACT.Copy, t, h_free)
                pending.append((k, h))
                if k % HB:
                    low_part()
                if k % HB == HB - 1:
                    low_part()
                return f
            product(True, hi, lo, kt, None, evac, by_k=ready)
        return ok

    lam1 = small(2)
    lt = small(HD)[0:1, :]
    for n, (a, c) in enumerate((("lq1", "lk1"), ("lq2", "lk2"))):
        t = tt(lt, rows[a], rows[c], MUL, vecs, ve.last)
        t = red(lam1[0:1, n:n + 1], lt, ADD, t)
    lam2 = small(2)
    t = act(lam2[0:1, :], lam1[0:1, :], ACT.Exp, t)
    lam3 = small(1)
    t = tt(lam3[0:1, :], lam2[0:1, 1:2], lam2[0:1, 0:1], SUB, t)
    lam_ok = ts(lam3[0:1, :], lam3[0:1, :], -LAM_INIT, None, ADD, None, t)

    g, g_ok = gates(bg, 0, w_free)
    m_ok = merge_first(yhi, ylo, KD, y_ok, g, g_ok, x_read)
    y_free = pe.last

    nlam = small(1)
    b, ps, bf = bank()
    tk = mm(ps[:, 0:1], ones[0:1, :], lam3[0:1, :], True, True, lam_ok, bf, signal=True)
    bank_free[b] = nlam_ok = cp(nlam, ps[:, 0:1], tk)
    sg8 = small(1)
    sg_ok = ts(sg8, sg, 1.0 - LAM_INIT, None, MUL, None, vecs)
    gq8 = {}
    for name in ("q1", "q2"):
        a = small(1)
        gq_ok = ts(a, halves[name], HD ** -0.5, None, MUL, None, vecs)
        gq8[name] = a

    dist = T[:, 0:BANK]
    spat_read = [y_ok[-1], pe.last, ve.last]
    dist_i = W[:, 3, 0:BANK].bitcast(I32)
    t = po.do(lambda e: e.iota(dist_i, pattern=[[1, BANK]], base=-(SEQ - P), channel_multiplier=-1), spat_read)
    t = cp(dist, dist_i, t, spat_read)
    dist_ok = po.do(lambda e: e.affine_select(out=dist, in_=dist, compare_op=ALU.is_ge, fill=NEG,
                                              base=SEQ - P, pattern=[[-1, BANK]], channel_multiplier=1), t)

    def turn_block(src, dst, gain, ready, free):
        s = src.rearrange("p (i n) -> p i n", i=NT)
        d = dst.rearrange("p (c n) -> p c n", c=HB)
        for c in range(HB):
            b, ps, bf = bank()
            for i in range(NT):
                tk = turn(ps[:, i * P:i * P + P], s[:, i, c * P:c * P + P], ready, bf, signal=i == NT - 1)
            t = bank_free[b] = act(d[:, c, :], ps, ACT.Copy, tk, free, gq_ok, vecs, scale=gain)
        return t, tk

    DEEP = 3
    S_ = T[:, 512:512 + DEEP * 1024].rearrange("p (u c n) -> p u c n", u=DEEP, c=2)
    SQ = T[:, 512:512 + UNIT]
    AT = T[:, 3584:3584 + 1024].rearrange("p (u n) -> p u n", u=2)
    BI = W[:, 3, 0:BANK]
    ON = W[:, 3, BANK:2 * BANK]
    ON2 = W[:, 3, 2 * BANK:3 * BANK]
    yb_ok = []
    s_free, at_free, bi_free, on_free = [None] * DEEP, [None] * 2, [None], [None]
    ring3 = small(DEEP, 16)
    qt, kt_ = W[:, 1, :], W[:, 2, :]
    qT = qt.rearrange("p (c n) -> p c n", c=HB)
    kT = kt_.rearrange("p (c n) -> p c n", c=HB)
    vN = W[:, 0, :].rearrange("p (i n) -> p i n", i=NT)
    gate_out, gate_stored = [Arrivals(sem(f"s_gate{i}")) for i in range(2)], []
    clear = [m_ok, dist_ok, t, yz_ok, g_ok]
    for b in range(2):
        vt = natural_block(W[:, 0, :], SQ, clear, clear)
        nq_ok = group_norm(W[:, 0, :], SQ, HD, vt)
        turned_q, turned_k = [], []
        kt2 = natural_block(W[:, 3, :], SQ, clear, nq_ok, between=lambda: turned_q.extend(
            turn_block(W[:, 0, :], qt, gq8["q1"], nq_ok, clear)))
        nk_ok = group_norm(W[:, 3, :], SQ, HD, kt2)
        q_ok, q_rd = turned_q
        v_ok = natural_block(W[:, 0, :], None, [q_rd, nq_ok], between=lambda: turned_k.extend(
            turn_block(W[:, 3, :], kt_, halves["k1"], nk_ok, clear)))
        k_ok, k_rd = turned_k
        steps = [(h, i) for h in range(4) for i in range(NT)]
        st = {}
        heads_out = {}
        bi_ok = [None]
        w3_clear = [k_rd, nk_ok]

        def scores(n_it):
            h, i = steps[n_it]
            hh, u, n = b * 4 + h, n_it % DEEP, P * (i + 1)
            if i == 0:
                bi_ok[0] = ts(BI, dist, 2.0 ** (-8.0 * (hh + 1) / HEADS1), None, MUL, None, dist_ok,
                              bi_free[0], w3_clear)
            for c in range(2):
                bb, ps, bf = bank()
                tk = mm(ps[:, 0:n], qT[64 * c:64 * c + 64, h, i * P:i * P + P],
                        kT[64 * c:64 * c + 64, h, 0:n], True, True, q_ok, k_ok, bf, signal=True)
                t = tt(S_[:, u, c, 0:n], ps[:, 0:n], BI[:, BANK - n:BANK], ADD, tk, bi_ok[0],
                       s_free[u], nk_ok)
                bank_free[bb] = bi_free[0] = t
            st[n_it] = red(ring3[:, u, 0:2], S_[:, u, :, 0:n], MAX, t, neg=True)

        def exponentials(n_it):
            h, i = steps[n_it]
            u, n = n_it % DEEP, P * (i + 1)
            sm = ring3[:, u, :]
            for c in range(2):
                t = act(S_[:, u, c, 0:n], S_[:, u, c, 0:n], ACT.Exp, st[n_it], bias=sm[:, c:c + 1],
                        acc=sm[:, 2 + c:3 + c])
            st[n_it] = t

        def combine(n_it):
            h, i = steps[n_it]
            u, n = n_it % DEEP, P * (i + 1)
            sm = ring3[:, u, :]
            t = ve.do(lambda e: e.reciprocal(sm[:, 4:6], sm[:, 2:4]), st[n_it])
            t = tt(sm[:, 6:7], sm[:, 5:6], nlam, MUL, t, nlam_ok)
            t = ts(S_[:, u, 1, 0:n], S_[:, u, 1, 0:n], sm[:, 6:7], None, MUL, None, t)
            st[n_it] = stt(S_[:, u, 0, 0:n], S_[:, u, 0, 0:n], sm[:, 4:5], S_[:, u, 1, 0:n], MUL, ADD, t)

        def turn_weights(n_it):
            h, i = steps[n_it]
            u, n = n_it % DEEP, P * (i + 1)
            bb, ps, bf = bank()
            for k in range(i + 1):
                tk = turn(ps[:, k * P:k * P + P], S_[:, u, 0, k * P:k * P + P], st[n_it], bf, signal=k == i)
            s_free[u] = tk
            st[n_it] = bank_free[bb] = act(AT[:, n_it % 2, 0:n], ps[:, 0:n], ACT.Copy, tk,
                                           at_free[n_it % 2])

        def times_v(n_it):
            h, i = steps[n_it]
            u = n_it % 2
            if i == 0:
                heads_out[h] = bank()
            ob, ops, obf = heads_out[h]
            for k in range(i + 1):
                tk = mm(ops[:, i * P:i * P + P], AT[:, u, k * P:k * P + P], vN[:, k, h * P:h * P + P],
                        k == 0, k == i, st[n_it], v_ok, obf, signal=k == i)
            at_free[u] = tk
            if i < NT - 1:
                return
            o3 = ops.rearrange("p (i n) -> p i n", i=NT)
            sq = ON2.rearrange("p (i n) -> p i n", i=NT)
            ssn = small(NT)
            t = act(sq, o3, ACT.Square, tk, on_free[0], w3_clear)
            t = red(ssn, sq, ADD, t)
            r, rt = inverse_rms(ssn, NT, DV1, t)
            st["out", h] = bank_free[ob] = tt(ON.rearrange("p (i n) -> p i n", i=NT), o3,
                                              bc(r, [P, NT, P]), MUL, rt, on_free[0])

        def finish(n_it):
            h, i = steps[n_it]
            if i < NT - 1:
                return
            hh = b * 4 + h
            bb, ps, bf = bank()
            for i in range(NT):
                on_free[0] = turn(ps[:, i * P:i * P + P], ON[:, i * P:i * P + P], st["out", h], bf,
                                  signal=i == NT - 1)
            th = act(yhi[:, hh, :], ps, ACT.Copy, on_free[0], y_free, sg_ok, scale=sg8)
            t = bank_free[bb] = stt(ylo[:, hh, :], ps, sg8, as_f32(yhi[:, hh, :]), MUL, SUB, th)
            yb_ok.append(t)

        def evac_gate(c, ps, tok):
            k = b * HB + c
            t = act(merge_tmp[:, k % 2, :], ps, ACT.Copy, tok, gate_stored[-2] if k > 1 else clear)
            gate_stored.append(gate_out[k % 2].start(sp, gate_dram[k], merge_tmp[:, k % 2, :], t))
            return t

        beside = product_steps(hthi, htlo, KD, ht_ok, evac_gate)
        stages = ((scores, 0), (beside, 1), (turn_weights, 2), (times_v, 3), (beside, 1), (exponentials, 1),
                  (combine, 1), (finish, 5))
        for n in range(len(steps) + 5):
            for stage, behind in stages:
                if stage is beside:
                    next(beside, None)
                elif 0 <= n - behind < len(steps):
                    stage(n - behind)
        for _ in beside:
            pass
        clear = [pe.last, ve.last, ac.last]

    wr = T[:, 0:KD * (NG + NE)].rearrange("p (k n) -> p k n", k=KD)
    wr_in = Arrivals(sem("s_wr"))
    wr_in.start(sp, wr[:, :, 0:NG], w_rg[0].rearrange("(k p) n -> p k n", p=P), pe.last, ve.last)
    wr_ok = wr_in.start(sp, wr[:, :, NG:], w_re[0].rearrange("(k p) n -> p k n", p=P))

    g = W[:, 0:2, :].rearrange("p a n -> p (a n)").rearrange("p (k n) -> p k n", k=KD)
    gate_in, g_ok = Arrivals(sem("s_gate_back")), []
    t = gate_in.start(sp, g, gate_dram.rearrange("k p n -> p k n"), gate_stored[-2:], pe.last, ve.last)
    for k in range(KD):
        g_ok.append(act(g[:, k, :], g[:, k, :], ACT.Sigmoid, t, vecs, bias=bg[:, KD + k:KD + k + 1]))
    parts = merge_second(yhi, ylo, KD, yb_ok, g, g_ok, m_ok)
    xw = W[:, 2:4, :].rearrange("p a n -> p (a n)").rearrange("p (i d) -> p i d", i=NT)
    x_ok = x_in.start(sp, xw, xv, pe.last, ve.last)
    x1 = m_all[:, :].rearrange("p (i d) -> p i d", i=NT)
    x1_ok = [None] * NT
    for b in range(2):
        def evac(c, ps, tok):
            cols = slice(b * BANK, b * BANK + BANK)
            x1_ok[c] = tt(x1[:, c, cols], ps, xw[:, c, cols], ADD, tok, x_ok, parts)
            return x1_ok[c]
        product(False, hthi, htlo, KD, None, evac, by_k=parts)

    h2t = W[:, 2:4, :].rearrange("p a n -> p (a n)").rearrange("p (k n) -> p k n", k=KD)
    lb, lps, lbf = bank()
    lgt = W[0:NG + NE, 3, 0:SEQ]

    def router_tile(k, ok):
        mm(lps[0:NG + NE, :], wr[:, k, :], h2t[:, k, :], k == 0, False, ok, wr_ok, lbf)
    xs_toks, h2_ok, xs_read = normalise(m_all[:, :], x1_ok, [parts[-1]], g2, keep=h2t, each=router_tile)
    for i in range(NT):
        tk = mm(lps[0:NG + NE, i * P:i * P + P], router_bias, ones[0:1, :], False, i == NT - 1, vecs,
                signal=i == NT - 1)
    t = bank_free[lb] = cp(lgt, lps[0:NG + NE, :], tk)
    b, ps, bf = bank()
    lgp = ps.rearrange("p (i n) -> p i n", i=NT)
    for i in range(NT):
        tk = turn(lgp[:, i, 0:NG + NE], lgt[:, i * P:i * P + P], t, bf, signal=i == NT - 1)
    xs = W[:, 0:2, :].rearrange("p a n -> p (a n)").rearrange("p (i d) -> p i d", i=NT)
    xn_out = Arrivals(sem("s_xn"))
    xn_ok = xn_out.start(sp, xn_dram.rearrange("(i p) d -> p i d", p=P), xs, xs_toks)
    t_free = [ve.last, pe.last, ac.last]
    tcur = [BANK]

    def tmp_(*shape):
        n = 1
        for s_ in shape:
            n *= s_
        a = T[:, tcur[0]:tcur[0] + n]
        tcur[0] += n
        assert tcur[0] <= 5632
        if len(shape) == 2:
            return a.rearrange("p (a b) -> p a b", b=shape[1])
        if len(shape) == 3:
            return a.rearrange("p (a b c) -> p a b c", b=shape[1], c=shape[2])
        return a

    h2t_read = tk
    lg = tmp_(NT, NG + NE)
    t = bank_free[b] = cp(lg, lgp[:, :, 0:NG + NE], tk, t_free)
    NTILE = NE + EXTRA
    assert NE <= CAP and NTILE <= CAP
    iot_i = SI[:, 0:CAP]
    count_up = tmp_(CAP)
    eidx = count_up[:, 0:NE]
    ti = po.do(lambda e: e.iota(iot_i, pattern=[[1, CAP]], base=0, channel_multiplier=0))
    t = cp(count_up, iot_i, ti, t)

    def first_of(values, best, n, tok):
        oh, rk, bk = tmp_(NT, n), tmp_(NT, n), tmp_(NT)
        t = tt(oh, values, bc(best, [P, NT, n]), ALU.is_equal, tok)
        w8 = tmp_(n)
        t = ts(w8, eidx[:, 0:n], -1.0, float(n), MUL, ADD, t)
        t = tt(rk, oh, w8.unsqueeze(1).broadcast_to([P, NT, n]), MUL, t)
        t = red(bk, rk, MAX, t)
        return oh, tt(oh, rk, bc(bk, [P, NT, n]), ALU.is_equal, t)

    mx = tmp_(NT)
    t = red(mx, lg[:, :, 0:NG], MAX, t)
    ohg, t = first_of(lg[:, :, 0:NG], mx, NG, t)
    ex = tmp_(NT, NG)
    t = tt(ex, lg[:, :, 0:NG], bc(mx, [P, NT, NG]), SUB, t)
    t = act(ex, ex, ACT.Exp, t)
    gs, gate = tmp_(NT), tmp_(NT)
    t = red(gs, ex, ADD, t)
    t = ve.do(lambda e: e.reciprocal(gate, gs), t)
    sel = tmp_(NT, NE)
    by_group = lambda a: a.rearrange("p i (g e) -> p i g e", g=NG)
    t = tt(by_group(sel), by_group(lg[:, :, NG:]), bc(ohg, [P, NT, NG, EPG]), MUL, t)
    el = tmp_(NT, EPG)
    t = red(el, sel.rearrange("p i (g e) -> p i e g", g=NG), ADD, t)
    m1, m2 = tmp_(NT), tmp_(NT)
    t = red(m1, el, MAX, t)
    oh1, t = first_of(el, m1, EPG, t)
    el2 = tmp_(NT, EPG)
    t = stt(el2, oh1, NEG, el, MUL, ADD, t)
    t = red(m2, el2, MAX, t)
    oh2, t = first_of(el2, m2, EPG, t)
    wt = tmp_(2, NT)
    p2, den = tmp_(NT), tmp_(NT)
    t = tt(p2, m2, m1, SUB, t)
    t = act(p2, p2, ACT.Exp, t)
    t = ts(den, p2, 1.0, None, ADD, None, t)
    t = ve.do(lambda e: e.reciprocal(den, den), t)
    t = tt(wt[:, 0, :], den, gate, MUL, t)
    t = tt(wt[:, 1, :], wt[:, 0, :], p2, MUL, t)
    E = [tmp_(NT, NE), tmp_(NT, NE)]
    for n, oh in enumerate((oh1, oh2)):
        t = tt(by_group(E[n]), bc(ohg, [P, NT, NG, EPG]), oh.unsqueeze(2).broadcast_to([P, NT, NG, EPG]), MUL, t)
    both = tmp_(NT, NE)
    t = tt(both, E[0], E[1], ADD, t)
    b, ps, bf = bank()
    rp = ps[:, 0:(NT + 1) * NE].rearrange("p (i e) -> p i e", i=NT + 1)
    for i in range(NT + 1):
        for j in range(min(i + 1, NT)):
            last = j == min(i, NT - 1)
            tk = mm(rp[:, i, :], upper if j == i else ones, both[:, j, :], j == 0, last, t, const_ok, bf,
                    signal=last)
    rank, cnt = tmp_(NT, NE), tmp_(NE)
    t = cp(rank, rp[:, 0:NT, :], tk)
    t = bank_free[b] = cp(cnt, rp[:, NT, :], t)
    xtra, tmpe = tmp_(NE), tmp_(NE)
    MAXC = SEQ // CAP
    t = ts(xtra, cnt, float(CAP), None, ALU.is_gt, None, t)
    for m in range(2, MAXC):
        t = stt(xtra, cnt, float(CAP * m), xtra, ALU.is_gt, ADD, t)
    inc = [tmp_(NE), tmp_(NE)]
    t = cp(inc[0], xtra, t)
    cur, step = 0, 1
    while step < NE:
        t = cp(inc[1 - cur][:, 0:step], inc[cur][:, 0:step], t)
        t = tt(inc[1 - cur][:, step:], inc[cur][:, step:], inc[cur][:, 0:NE - step], ADD, t)
        cur, step = 1 - cur, 2 * step
    incl = inc[cur]
    off = tmp_(NE)
    t = tt(off, incl, xtra, SUB, t)
    slot = tmp_(2, NT)
    toki = SI[:, 64:64 + NT]
    ti = po.do(lambda e: e.iota(toki, pattern=[[P, NT]], base=0, channel_multiplier=1))
    base0, base1 = tmp_(NE), tmp_(NE)
    t = ts(base0, eidx, float(CAP), None, MUL, None, t)
    t = ts(base1, off, float(CAP), float(CAP * (NE - 1)), MUL, ADD, t)
    prod, r1, a0, a1, far = tmp_(NT, NE), tmp_(NT), tmp_(NT), tmp_(NT), tmp_(NT)
    for n in range(2):
        for src, dst in ((rank, r1), (base0.unsqueeze(1).broadcast_to([P, NT, NE]), a0),
                         (base1.unsqueeze(1).broadcast_to([P, NT, NE]), a1)):
            t = tt(prod, E[n], src, MUL, t)
            t = red(dst, prod, ADD, t)
        t = ts(far, r1, float(CAP), None, ALU.is_ge, None, t)
        t = tt(a1, a1, a0, SUB, t)
        t = tt(a1, a1, far, MUL, t)
        t = tt(a0, a0, a1, ADD, t)
        t = tt(slot[:, n, :], a0, r1, ADD, t)
    slot_i = SI[:, 72:72 + 2 * NT]
    slot_u = slot_i.bitcast(U32)
    slot_ok = cp(slot_i, slot.rearrange("p a b -> p (a b)"), t)
    shift = CAP.bit_length() - 1
    tile_i, place_i = SI[:, 96:96 + 2 * NT], SI[:, 112:112 + 2 * NT]
    t = ts(tile_i, slot_i, shift, None, ALU.arith_shift_right, None, slot_ok)
    t = ts(place_i, slot_i, CAP - 1, None, ALU.bitwise_and, None, t)
    tile_f, place_f, tok_f = tmp_(2 * NT), tmp_(2 * NT), tmp_(NT)
    t = cp(tile_f, tile_i, t)
    t = cp(place_f, place_i, t)
    t = cp(tok_f, toki, t, ti)
    is_place, is_tile = tmp_(2 * NT, CAP), tmp_(2 * NT, NTILE)
    val = tmp_(2 * NT, 2 * NTILE)
    t = tt(is_place, count_up.unsqueeze(1).broadcast_to([P, 2 * NT, CAP]), bc(place_f, [P, 2 * NT, CAP]),
           ALU.is_equal, t)
    t = tt(is_tile, count_up[:, 0:NTILE].unsqueeze(1).broadcast_to([P, 2 * NT, NTILE]),
           bc(tile_f, [P, 2 * NT, NTILE]), ALU.is_equal, t)
    for n in range(2):
        of = slice(n * NT, (n + 1) * NT)
        t = tt(val[:, of, 0:NTILE], is_tile[:, of], bc(tok_f, [P, NT, NTILE]), MUL, t)
    t = tt(val[:, :, NTILE:], is_tile, bc(wt.rearrange("p a b -> p (a b)"), [P, 2 * NT, NTILE]), MUL, t)
    b, ps, bf = bank()
    for n in range(2 * NT):
        tk = mm(ps[0:CAP, 0:2 * NTILE], is_place[:, n, :], val[:, n, :], n == 0, n == 2 * NT - 1, t, bf,
                signal=n == 2 * NT - 1)
    info = small(2, NTILE)[0:CAP]
    idx = sb("slot_tokens", [CAP, NTILE], U32)
    t = bank_free[b] = cp(info.rearrange("p c n -> p (c n)"), ps[0:CAP, 0:2 * NTILE], tk)
    t = idx_ok = cp(idx[:, :], info[:, 0, :], t)
    ovf, ovn = tmp_(EXTRA, NE), tmp_(EXTRA)
    t = tt(ovf, incl.unsqueeze(1).broadcast_to([P, EXTRA, NE]), bc(count_up[:, 0:EXTRA], [P, EXTRA, NE]),
           ALU.is_le, t)
    t = red(ovn, ovf, ADD, t)
    t = ts(ovn, ovn, float(NE - 1), None, MIN, None, t)
    ov_ids = SI[:, 80:80 + EXTRA + 1]
    t = cp(ov_ids[:, 0:EXTRA], ovn, t)
    ov_ok = cp(ov_ids[:, EXTRA:EXTRA + 1], incl[:, NE - 1:NE], t)


    XG = W[0:CAP, 0:2, :].rearrange("p a n -> p (a n)")[:, 0:3 * D].rearrange("p (u d) -> p u d", u=3)
    YO = W[0:CAP, 2, :].rearrange("p (u d) -> p u d", u=2)
    HF = W[:, 3, 0:BANK].rearrange("p (k n) -> p k n", k=KD)
    SG = W[0:CAP, 3, 512:512 + 2 * DE].rearrange("p (u n) -> p u n", u=2)
    HID = W[0:CAP, 3, 1024:1024 + 2 * DE].rearrange("p (u n) -> p u n", u=2)
    GHI = yhi[:, 0:2, :].rearrange("p u (k n) -> p u k n", k=KD)
    GLO = ylo[:, 0:2, :].rearrange("p u (k n) -> p u k n", k=KD)
    HHI = yhi[:, 2, 0:4 * CAP].rearrange("p (u k n) -> p u k n", u=2, k=2)
    HLO = ylo[:, 2, 0:4 * CAP].rearrange("p (u k n) -> p u k n", u=2, k=2)
    xg_in = [Arrivals(sem(f"s_xg{i}")) for i in range(3)]
    y_out = [Arrivals(sem(f"s_yo{i}")) for i in range(2)]
    xg_ok, xg_free = {}, [[xs_read, xn_ok, ve.last]] * 3
    g_split, h_split, g_free, hid_ok, h_free, yo_free = {}, {}, [[y_free, pe.last]] * 2, {}, [None] * 2, [None] * 2
    w_clear = [h2t_read, xn_ok]
    dk = [None]

    def gather(e):
        u = e % 3
        xg_ok[e] = xg_in[u].start_indirect(po, lambda q: q.indirect_dma_start(
            out=XG[:, u, :], out_offset=None, in_=xn_dram,
            in_offset=bass.IndirectOffsetOnAxis(ap=idx[:, e:e + 1], axis=0)), idx_ok, xg_free[u], xn_ok)

    def bring(e):
        u = e % 2
        b, ps, bf = bank()
        pv = ps.rearrange("p (k n) -> p k n", k=KD)
        for k in range(KD):
            tk = turn(pv[:, k, :], XG[:, e % 3, k::KD], xg_ok[e], bf, signal=k == KD - 1)
        xg_free[e % 3] = tk
        t = bank_free[b] = tt(HF, pv, bc(g2p, [P, KD, CAP]), MUL, tk, vecs, w_clear, dk[0])
        h = act(GHI[:, u], HF, ACT.Copy, t, g_free[u])
        dk[0] = g_split[e] = tt(GLO[:, u], HF, as_f32(GHI[:, u]), SUB, h, g_free[u])

    def hand_over(e):
        u = e % 2
        b, ps, bf = bank()
        pv = ps[:, 0:2 * CAP].rearrange("p (k n) -> p k n", k=2)
        for k in range(2):
            tk = turn(pv[:, k, :], HID[:, u, k::2], hid_ok[e], bf, signal=k == 1)
        h_free[u] = tk
        h = act(HHI[:, u], pv, ACT.Copy, tk)
        h_split[e] = bank_free[b] = tt(HLO[:, u], pv, as_f32(HHI[:, u]), SUB, h)

    def up(e):
        u = e % 2
        b, ps, bf = bank()
        for kh in range(2):
            j, wh, wl, ok = take()
            wh, wl = (a.rearrange("p (j k f) -> p j k f", j=2, k=HB) for a in (wh, wl))
            for k in range(HB):
                kk = kh * HB + k
                tk = passes(ps[0:CAP, :], GHI[:, u, kk, :], GLO[:, u, kk, :], wh[:, :, k, :], wl[:, :, k, :],
                            kk == 0, kk == KD - 1, ok, g_split[e], bf, signal=k == HB - 1)
            done(j, tk, more=kh == 0)
        g_free[u] = tk
        ta = act(SG[:, u, :], ps[0:CAP, 0:DE], ACT.Sigmoid, tk, h_free[u], w_clear)
        t = tt(SG[:, u, :], SG[:, u, :], ps[0:CAP, 0:DE], MUL, ta)
        t = stt(HID[:, u, :], SG[:, u, :], info[:, 1, e:e + 1], ps[0:CAP, DE:2 * DE], MUL, MUL, t, h_free[u])
        bank_free[b] = hid_ok[e] = t
        split_more(split[0] + len(slots))

    def down(e):
        u = e % 2
        j, wh, wl, ok = take()
        wh, wl = (a.rearrange("p (k n) -> p k n", k=2) for a in (wh, wl))
        held = [bank(), bank()]
        toks = []
        for half in range(2):
            cols = slice(half * BANK, half * BANK + BANK)
            for k in range(2):
                tk = passes(held[half][1][0:CAP, :], HHI[:, u, k, :], HLO[:, u, k, :], wh[:, k, cols],
                            wl[:, k, cols], k == 0, k == 1, ok, h_split[e], held[half][2], signal=k == 1)
            toks.append(tk)
        done(j, tk, more=False)
        for half in range(2):
            cols = slice(half * BANK, half * BANK + BANK)
            t = bank_free[held[half][0]] = act(YO[:, u, cols], held[half][1][0:CAP, :], ACT.Copy,
                                               toks[half], yo_free[u], w_clear)
        yo_free[u] = y_out[u].start(ac, y_dram[e * CAP:(e + 1) * CAP, :], YO[:, u, :], t)

    slots.extend((NS + n, [pe.last, y_free]) for n in range(LENT_SPLIT))
    raw_slots.extend((NR + n, [ve.last, ac.last, pe.last, idx_ok, ov_ok]) for n in range(LENT_RAW))
    load_more(len(units))
    gather(0)
    gather(1)
    bring(0)
    split_more(split[0] + len(slots))
    for e in range(NE + 1):
        if e + 2 < NE:
            gather(e + 2)
        if e + 1 < NE:
            bring(e + 1)
        if e:
            hand_over(e - 1)
        split_more(split[0] + len(slots))
        if e < NE:
            up(e)
        if e:
            down(e - 1)

    main_end = [q.last for q in (pe, ve, ac, po)] + yo_free + [yz_ok]
    names = ("pe", "ve", "ac", "po", "sp")
    ope, ove, oac, opo, osp = (Queue(sem(f"s_over_{n}")) for n in names)
    o_in, o_w, o_y = (Arrivals(sem(f"s_over_{n}")) for n in ("in", "w", "y"))
    w13 = W[:, 0:2, :].rearrange("p a n -> p (a n)").rearrange("p (j k f) -> p j k f", j=2, k=KD)
    wdn = W[:, 2, :].rearrange("p (k n) -> p k n", k=2)
    oxg = W[0:CAP, 3, 0:D]
    ogt = W[:, 3, D:D + BANK].rearrange("p (k n) -> p k n", k=KD)
    osg = W[0:CAP, 3, D + BANK:D + BANK + DE]
    oht = W[:, 3, D + BANK + DE:D + BANK + DE + 2 * CAP].rearrange("p (k n) -> p k n", k=2)
    OVB = [PS[:, n, :] for n in range(4)]
    w_load = {}
    end = None
    for j in range(EXTRA):
        tile = NE + j
        def from_id(e, j=j):
            w_load[j] = e.value_load(ov_ids[0:1, j:j + 1], min_val=0, max_val=NE - 1)
        osp.quiet(from_id, end)
        for n, (dst, src) in enumerate(((w13[:, 0], w1), (w13[:, 1], w3), (wdn, w2))):
            osp.wait(end)
            o_w.count += 16
            def load(e, j=j, dst=dst, src=src):
                v = w_load[j]
                k = dst.shape[1]
                e.dma_start(dst, src[0, bass.ds(v, 1)].rearrange("o (p k) f -> (o p) k f", k=k)).then_inc(o_w.sem, 16)
            osp.steps.append(load)
        w_ok = (o_w.sem, o_w.count)
        x_got = o_in.start_indirect(opo, lambda q, tile=tile: q.indirect_dma_start(
            out=oxg, out_offset=None, in_=xn_dram,
            in_offset=bass.IndirectOffsetOnAxis(ap=idx[:, tile:tile + 1], axis=0)), end)
        pv = OVB[0].rearrange("p (k n) -> p k n", k=KD)
        for k in range(KD):
            make = lambda e, k=k: e.transpose(pv[:, k, :], oxg[:, k::KD], ident[0:CAP, 0:CAP])
            tk = ope.do(make, x_got, end)
        t = ove.do(lambda e: e.tensor_tensor(ogt, pv, bc(g2p, [P, KD, CAP]), MUL), tk)
        for k in range(KD):
            tk = ope.do(lambda e, k=k: e.matmul(OVB[1][0:CAP, :], ogt[:, k, :], w13[:, :, k, :], start=k == 0,
                                                stop=k == KD - 1), t, w_ok)
        t = oac.do(lambda e: e.activation(osg, OVB[1][0:CAP, 0:DE], ACT.Sigmoid), tk)
        t = ove.do(lambda e: e.tensor_tensor(osg, osg, OVB[1][0:CAP, 0:DE], MUL), t)
        t = ove.do(lambda e, tile=tile: e.scalar_tensor_tensor(
            osg, osg, info[:, 1, tile:tile + 1], OVB[1][0:CAP, DE:2 * DE], MUL, MUL), t)
        pv2 = OVB[0][:, 0:2 * CAP].rearrange("p (k n) -> p k n", k=2)
        for k in range(2):
            tk = ope.do(lambda e, k=k: e.transpose(pv2[:, k, :], osg[:, k::2], ident[0:CAP, 0:CAP]), t)
        t = ove.do(lambda e: e.tensor_copy(oht, pv2), tk)
        for half in range(2):
            cols = slice(half * BANK, half * BANK + BANK)
            for k in range(2):
                tk = ope.do(lambda e, half=half, k=k, cols=cols: e.matmul(
                    OVB[2 + half][0:CAP, :], oht[:, k, :], wdn[:, k, cols], start=k == 0, stop=k == 1), t)
        for half in range(2):
            cols = slice(half * BANK, half * BANK + BANK)
            t = ove.do(lambda e, half=half, cols=cols: e.tensor_copy(oxg[:, cols], OVB[2 + half][0:CAP, :]), tk)
        end = o_y.start(osp, y_dram[tile * CAP:(tile + 1) * CAP, :], oxg, t)
    over = dict(pe=ope, ve=ove, ac=oac, po=opo, sp=osp)
    for q in over.values():
        q.wait(end)

    def branch(queue, name):
        def step(e):
            v = e.value_load(ov_ids[0:1, EXTRA:EXTRA + 1], min_val=0, max_val=EXTRA)
            with e.If(v):
                over[name].play(e)
        queue.quiet(step, main_end, ov_ok)

    for q, name in zip((pe, ve, ac, po, sp), names):
        branch(q, name)

    lent = [s for s in slots if s[0] >= NS]
    assert len(lent) == LENT_SPLIT
    for s in lent:
        slots.remove(s)
    lent = [s for s in raw_slots if s[0] >= NR]
    assert len(lent) == LENT_RAW
    for s in lent:
        raw_slots.remove(s)
    fetch = [Arrivals(sem(f"s_fetch{i}")) for i in range(4)]
    YG = W[:, :, :].rearrange("p u (a d) -> p u a d", a=2)
    x2_out = Arrivals(sem("s_x2"))
    x2_ok = []
    for i in range(NT):
        for n in range(2):
            f_ok = fetch[i].start_indirect(po, lambda q, i=i, n=n: q.indirect_dma_start(
                out=YG[:, i, n, :], out_offset=None, in_=y_dram,
                in_offset=bass.IndirectOffsetOnAxis(ap=slot_u[:, n * NT + i:n * NT + i + 1], axis=0)))
        t = tt(YG[:, i, 0, :], YG[:, i, 0, :], YG[:, i, 1, :], ADD, f_ok)
        t = tt(x1[:, i, :], x1[:, i, :], YG[:, i, 0, :], ADD, t)
        x2_ok.append(t)
    for i in range(NT):
        x2_stored = x2_out.start(sp, x2_dram[i * P:i * P + P, :], x1[:, i, :], x2_ok)
    def block_two():
        _, h_ok, xs_rd = normalise(m_all[:, :], x2_ok, [ve.last, pe.last], g3)
        m_free = [x2_stored, ve.last, ac.last]
        t_clear = [ve.last, ac.last, pe.last]
        NAT = W[:, 0:3, :].rearrange("p a n -> p (a n)").rearrange("p (i n) -> p i n", i=NT)

        ii, jj = T[:, 0:P].bitcast(I32), T[:, P:2 * P].bitcast(I32)
        xr, sh = T[:, 2 * P:3 * P].bitcast(I32), T[:, 3 * P:4 * P].bitcast(I32)
        shf = T[:, 4 * P:5 * P]
        ti = po.do(lambda e: e.iota(ii, pattern=[[1, P]], base=0, channel_multiplier=0), t_clear)
        ti = po.do(lambda e: e.iota(jj, pattern=[[0, P]], base=0, channel_multiplier=1), t_clear)
        t = tt(xr, ii, jj, ALU.bitwise_xor, ti)
        LEVELS = 6
        level = []
        for l in range(LEVELS + 1):
            t = ts(sh, xr, l, None, ALU.arith_shift_right, None, t)
            t = cp(shf, sh, t)
            a = const(P)
            if l < LEVELS:
                t = ts(a, shf, 1.0, None, ALU.is_equal, None, t)
                t = tt(a, a, upper, MUL, t)
                level.append(a)
            else:
                same = a
                t = ts(a, shf, 0.0, None, ALU.is_equal, None, t)
        causal = const(P)
        t = tt(causal, upper, ident, ADD, t)
        t = masks_ok = tt(causal, causal, same, MUL, t)

        load_limit[0] = unit_at[0] + 5 * (KD // HB)
        LEAD = TAPS - 1
        UB = T[:, 1024:1024 + 2 * (SEQ + 4)].rearrange("p (u n) -> p u n", u=2)
        SGB = T[:, 2560:2560 + 2 * SEQ].rearrange("p (u n) -> p u n", u=2)
        CV = W[:, 3, :].rearrange("p (c n) -> p c n", c=HB)
        zt = None
        for u in range(2):
            zt = ve.do(lambda e, u=u: e.memset(UB[:, u, 0:LEAD], 0.0), t_clear, zt)
        ub_free, sg_free, cv_free, cv_ok = [zt, zt], [t_clear] * 2, [t_clear] * HB, {}
        nat_ok = []

        def to_natural(blk):
            def run():
                for c in range(HB):
                    ch = blk * HB + c
                    b, ps, bf = bank()
                    for i in range(NT):
                        tk = turn(ps[:, i * P:i * P + P], CV[:, c, i * P:i * P + P], cv_ok[ch], bf,
                                  signal=i == NT - 1)
                    cv_free[c] = tk
                    bank_free[b] = act(NAT[:, :, ch * P:ch * P + P], ps.rearrange("p (i n) -> p i n", i=NT),
                                       ACT.Copy, tk, xs_rd)
                    nat_ok.append(bank_free[b])
            return run

        unfinished = []

        def silu(ch, u, a, t):
            g_ = act(SGB[:, u, :], a, ACT.Sigmoid, t, sg_free[u])
            cv_ok[ch] = sg_free[u] = tt(a, a, SGB[:, u, :], MUL, g_)

        for blk in range(3):
            def evac(c, ps, tok):
                ch, u = blk * HB + c, c % 2
                f = act(UB[:, u, LEAD:LEAD + SEQ], ps, ACT.Copy, tok, ub_free[u])
                a = CV[:, c, :]
                t = ts(a, UB[:, u, LEAD:LEAD + SEQ], cw[:, ch, LEAD:LEAD + 1], None, MUL, None, f,
                       cv_free[c], vecs)
                for k in range(LEAD):
                    t = stt(a, UB[:, u, k:k + SEQ], cw[:, ch, k:k + 1], a, MUL, ADD, t)
                ub_free[u] = t
                unfinished.append((ch, u, a, t))
                while len(unfinished) > (c < HB - 1):
                    silu(*unfinished.pop(0))
                return f
            product(True, hthi, htlo, KD, h_ok, evac, between=to_natural(blk - 1) if blk else None)

        t = wba_ok
        b, ps, bf = bank()
        for k in range(KD):
            tk = passes(ps[0:NB, :], wbah[:, k, :], wbal[:, k, :], hthi[:, k, :], htlo[:, k, :], k == 0,
                        k == KD - 1, t, h_ok, bf, signal=k == KD - 1)
        bat = T[0:NB, 3584:3584 + SEQ]
        bat_ok = bank_free[b] = act(bat, ps[0:NB, :], ACT.Copy, tk)
        ba = small(NT, NB)
        b, ps, bf = bank()
        mm(ps[:, 0:DH], ones[0:1, :], rows["dtb"], True, True, vecs, bf)
        tk = mm(ps[:, DH:2 * DH], ones[0:1, :], rows["alog"], True, True, signal=True)
        dta = small(2 * DH)
        t2 = bank_free[b] = cp(dta, ps[:, 0:2 * DH], tk)
        N16 = NT * DH
        by_tile = lambda a, i: a[:, i * DH:(i + 1) * DH]
        beta_ok = eg_ok = qk_ok = tprev = None
        beta, gl, ab, ea = small(NT, DH), small(NT, DH), small(NT, DH), small(DH)
        egc, edl = small(N16), small(N16)
        gend = small(2 * N16)
        sums = small(4 * N16)
        gflat = gl.rearrange("p a b -> p (a b)")
        gc = sums[:, 0:N16]
        betaf = beta.rearrange("p a b -> p (a b)")

        def decays():
            nonlocal beta_ok, eg_ok
            beta_ok = act(beta, ba[:, :, 0:DH], ACT.Sigmoid, t1)
            t = tt(gl, ba[:, :, DH:], dta[:, 0:DH].unsqueeze(1).broadcast_to([P, NT, DH]), ADD, t1, t2)
            t = act(ab, gl, ACT.Abs, t)
            t = act(ab, ab, ACT.Exp, t, scale=-1.0)
            t = act(ab, ab, ACT.Ln, t, bias=1.0)
            te = act(ea, dta[:, DH:], ACT.Exp, t2)
            t = stt(gl, gl, 0.0, ab, MAX, ADD, t)
            t = stt(gl, gl, -1.0, ea.unsqueeze(1).broadcast_to([P, NT, DH]), MUL, MUL, t, te)
            b, ps, bf = bank()
            mm(ps[:, 0:N16], causal, gflat, True, True, t, masks_ok, bf)
            mm(ps[:, N16:2 * N16], same, gflat, True, True, signal=True)
            for c in range(2):
                r_ = slice(64 * c, 64 * c + 64)
                tk = mm(ps[:, (2 + c) * N16:(3 + c) * N16], ones[r_, :], gflat[r_, :], True, True, pe.last,
                        signal=True)
            t = bank_free[b] = cp(sums, ps[:, 0:4 * N16], tk)
            t = tt(edl, sums[:, N16:2 * N16], gc, SUB, t)
            act(edl, edl, ACT.Exp, t)
            act(gend, sums[:, 2 * N16:], ACT.Exp, t)
            eg_ok = act(egc, gc, ACT.Exp, t)

        def lengths():
            nonlocal qk_ok, tprev
            sq = W[:, 3, :].rearrange("p (i n) -> p i n", i=NT)
            tprev = [cv_free, nat_ok]
            for n in range(2):
                part = NAT[:, :, n * NH:(n + 1) * NH]
                ssn = small(N16)
                t = act(sq, part, ACT.Square, tprev)
                t = red(ssn, W[:, 3, :].rearrange("p (g d) -> p g d", d=DK), ADD, t)
                tprev = t
                r, rt = inverse_rms(ssn, N16, 1.0, t)
                if n == 0:
                    rt = ts(r, r, DK ** -0.5, None, MUL, None, rt)
                for i in range(NT):
                    v4 = part[:, i, :].rearrange("p (h d) -> p h d", h=DH)
                    t = tt(v4, v4, bc(by_tile(r, i), [P, DH, DK]), MUL, rt, nat_ok)
            qk_ok = t

        ZA = m_all[:, 0:UNIT].rearrange("p (c n) -> p c n", c=HB)
        ZB = m_all[:, UNIT:2 * UNIT].rearrange("p (c n) -> p c n", c=HB)
        z_ok = []

        to_natural(2)()
        b, ps, bf = bank()
        for i in range(NT):
            tk = turn(ps[:, i * NB:(i + 1) * NB], bat[:, i * P:(i + 1) * P], bat_ok, bf, signal=i == NT - 1)
        t1 = bank_free[b] = cp(ba, ps[:, 0:NT * NB].rearrange("p (i n) -> p i n", i=NT), tk)

        def first_between():
            decays()
            lengths()

        def evac_za(c, ps, tok):
            u = c % 2
            g_ = act(SGB[:, u, :], ps, ACT.Sigmoid, tok, sg_free[u])
            sg_free[u] = tt(ZA[:, c, :], ps, SGB[:, u, :], MUL, g_, m_free)
            z_ok.append(sg_free[u])
            return sg_free[u]
        product(True, hthi, htlo, KD, h_ok, evac_za, early=first_between)

        heads = lambda a: a.rearrange("p (h n) -> p h n", h=DH)
        places = [T[:, n * BANK:(n + 1) * BANK] for n in range(11)]
        places += [W[:, 3, n * BANK:(n + 1) * BANK] for n in range(4)]
        places += [raw[:, r, n * BANK:(n + 1) * BANK] for r in range(NR) for n in range(UNIT // BANK)]
        places = [heads(a) for a in places]
        S, vn = places.pop(0), places.pop(0)
        sets = [places[12:24], places[0:12]]
        s_ok = [ve.do(lambda e: e.memset(S, 0.0), tprev)]
        vn_free = [None]
        assert {s for s, _ in raw_slots} == set(range(NR))
        tiles_clear = [ve.last, pe.last, ac.last, *[tok for _, tok in raw_slots]]

        def turn4(dst, src, ready, free):
            b, ps, bf = bank()
            for h in range(DH):
                tk = turn(heads(ps)[:, h, :], src[:, h, :], ready, bf, signal=h == DH - 1)
            bank_free[b] = act(dst, heads(ps), ACT.Copy, tk, free)
            return bank_free[b], tk

        def mm4(l, r, *w):
            b, ps, bf = bank()
            for h in range(DH):
                tk = mm(heads(ps)[:, h, :], l[:, h, :], r[:, h, :], True, True, *w, bf, signal=h == DH - 1)
            return b, heads(ps), tk

        spread = lambda a, i: bc(by_tile(a, i), [P, DH, DK])
        each = lambda a: a.unsqueeze(1).broadcast_to([P, DH, P])
        o_ok = []

        def tile_steps(i, clear, out_):
            kT, kbT, qT, qdT, kd, dec, MT, TI, TT, qkT, nwT, GR = sets[i % 2]
            BT, Q, u_ = kT, kbT, qT
            Kn, Qn, Vn = (heads(NAT[:, i, n * NH:(n + 1) * NH]) for n in (1, 0, 2))
            kT_ok, k_rd = turn4(kT, Kn, qk_ok, clear)
            qT_ok, q_rd = turn4(qT, Qn, qk_ok, clear)
            kd_ok = tt(kd, Kn, spread(edl, i), MUL, eg_ok, clear, qk_ok)
            t = tt(Kn, Kn, spread(betaf, i), MUL, k_rd, beta_ok, kd_ok)
            yield
            kb_ok, kb_rd = turn4(kbT, Kn, t, clear)
            t = tt(GR, each(causal), spread(gflat, i), MUL, clear, masks_ok)
            b, ps, bf = bank()
            tk = mm(ps, ones, GR.rearrange("p h n -> p (h n)"), True, True, t, bf, signal=True)
            t = bank_free[b] = tt(dec, heads(ps), spread(gc, i), SUB, tk, clear)
            t = ts(dec, dec, 0.0, None, MIN, None, t)
            dec_ok = act(dec, dec, ACT.Exp, t)
            yield
            b, ps, tk = mm4(kT, kbT, kT_ok, kb_ok)
            m_ok_ = bank_free[b] = tt(MT, ps, dec, MUL, tk, dec_ok, clear)
            b, ps, tk = mm4(kT, qT, kT_ok, qT_ok)
            t = tt(BT, MT, each(level[0]), MUL, tk, m_ok_)
            t = tt_ok = tt(TT, each(ident), BT, SUB, t, clear)
            ti_ok, _ = turn4(TI, TT, t, clear)
            bt_ok = tt(BT, MT, each(level[1]), MUL, t)
            t = bank_free[b] = tt(qkT, ps, dec, MUL, tk, dec_ok, clear)
            qk2_ok = tt(qkT, qkT, each(causal), MUL, t)
            t = tt(Qn, Qn, spread(egc, i), MUL, q_rd, eg_ok)
            qd_ok, _ = turn4(qdT, Qn, t, clear)
            yield
            for l in range(1, LEVELS):
                b, ps, tk = mm4(BT, TI, bt_ok, ti_ok)
                q_ok2 = bank_free[b] = act(Q, ps, ACT.Copy, tk)
                if l < LEVELS - 1:
                    bt_ok = tt(BT, MT, each(level[l + 1]), MUL, tk)
                if l == 2:
                    rk_ok = tt(Kn, Kn, spread(egc, i), MUL, kb_rd, eg_ok)
                if l == 3:
                    bv_ok = tt(Vn, Vn, spread(betaf, i), MUL, beta_ok, nat_ok)
                yield
                b2, ps2, tk2 = mm4(Q, TT, q_ok2, tt_ok)
                if l < LEVELS - 1:
                    b, ps, tk = mm4(TT, Q, q_ok2, tt_ok)
                    ti_ok = bank_free[b] = tt(TI, TI, ps, SUB, tk, tk2, ti_ok)
                tt_ok = bank_free[b2] = tt(TT, TT, ps2, SUB, tk2, tk, tt_ok)
                yield
            b, ps, tk = mm4(Kn, TT, rk_ok, tt_ok)
            nw_ok = bank_free[b] = act(nwT, ps, ACT.Copy, tk, clear, scale=-1.0)
            b, ps, tk = mm4(TT, Vn, tt_ok, bv_ok)
            u_ok2 = bank_free[b] = cp(u_, ps, tk)
            yield "state"
            for c in range(2):
                R = slice(64 * c, 64 * c + 64)
                b, ps, tk = mm4(nwT, S, nw_ok, s_ok[0])
                v_ok2 = bank_free[b] = tt(vn[R], u_[R], ps[R], ADD, tk, u_ok2, vn_free[0], tiles_clear)
                yield
                b, ps, bf = bank()
                for h in range(DH):
                    tk = mm(heads(ps)[:, h, :], kd[R, h, :], vn[R, h, :], True, True, kd_ok, v_ok2, bf, signal=True)
                ge = gend[:, c * N16:(c + 1) * N16]
                bq, psq, bfq = bank()
                po_ = heads(psq)
                for h in range(DH):
                    mm(po_[:, h, :], qdT[:, h, :], S[:, h, :], True, False, qd_ok, s_ok[0], bfq)
                    tq = mm(po_[:, h, :], qkT[R, h, :], vn[R, h, :], False, True, qk2_ok, v_ok2, signal=True)
                vn_free[0] = tq
                t = tt(S, S, spread(ge, i), MUL, s_ok[0], tq, eg_ok)
                s_ok[0] = bank_free[b] = tt(S, S, heads(ps), ADD, t, tk)
                bank_free[bq] = act(Vn[R], po_[R], ACT.Copy, tq)
                o_ok.append(bank_free[bq])
                yield
            out_[i] = [ve.last, pe.last, ac.last]

        finished = {}

        def chain(first):
            clear = tiles_clear
            for i in range(first, NT, 2):
                for step in tile_steps(i, clear, finished):
                    while step == "state" and i and i - 1 not in finished:
                        yield
                    yield
                clear = finished[i]

        def evac_zb(c, ps, tok):
            zb_raw.append(act(ZB[:, c, :], ps, ACT.Copy, tok, m_free))
            return zb_raw[-1]

        zb_raw, zb_ok = [], []
        chains = [chain(0), chain(1), product_steps(hthi, htlo, KD, h_ok, evac_zb)]
        while chains:
            for c in list(chains):
                if next(c, "end") == "end":
                    chains.remove(c)
        clear = [ve.last, pe.last, ac.last]
        raw_slots[:] = [(s, finished[NT - 2]) for s in range(NR)]
        load_limit[0] = len(units)
        load_more(len(units))

        y_ok2, nat_free2 = [], []

        split_more(unit_at[0] + 1)
        O = NAT[:, :, 2 * NH:3 * NH]
        ssn = small(N16)
        sq_ = T[:, 0:UNIT]
        t = act(sq_.rearrange("p (i n) -> p i n", i=NT), O, ACT.Square, o_ok, clear)
        t = red(ssn, sq_.rearrange("p (g d) -> p g d", d=DK), ADD, t)
        r, rt = inverse_rms(ssn, N16, DK, t)
        for i in range(NT):
            v4 = heads(O[:, i, :])
            t = tt(v4, v4, bc(by_tile(r, i), [P, DH, DK]), MUL, rt, o_ok)
        o_rms_ok = t
        split_more(unit_at[0] + 2)

        def delta_output():
            tmp2 = T[:, UNIT:UNIT + 2 * BANK].rearrange("p (u n) -> p u n", u=2)
            for h in range(DH):
                b, ps, bf = bank()
                for i in range(NT):
                    tk = turn(ps[:, i * P:i * P + P], O[:, i, h * DK:h * DK + DK], o_rms_ok, bf, signal=i == NT - 1)
                tq = bank_free[b] = stt(tmp2[:, h % 2, :], ps, dng, ZA[:, h, :], MUL, MUL, tk, vecs, z_ok, y_ok2[-2:])
                y_ok2.append(split_act(yhi[:, h, :], ylo[:, h, :], tmp2[:, h % 2, :], tq))
            nat_free2.extend([tk, y_ok2[-1], ve.last])

        SQ2 = T[:, 0:UNIT]
        vt = natural_block(W[:, 0, :], SQ2, nat_free2, nat_free2, early=delta_output)
        nq_ok = group_norm(W[:, 0, :], SQ2, SBD, vt)
        turned_q, turned_k = [], []
        kt2 = natural_block(W[:, 3, :], SQ2, nat_free2, nq_ok, between=lambda: turned_q.extend(
            turn_block(W[:, 0, :], W[:, 1, :], gq8["q2"], nq_ok, nat_free2)))
        for c in range(HB):
            sgb = T[:, 3072 + c % 2 * BANK:3072 + (c % 2 + 1) * BANK]
            t = act(sgb, ZB[:, c, :], ACT.Sigmoid, zb_raw, y_ok2, zb_ok[-2:])
            zb_ok.append(tt(ZB[:, c, :], ZB[:, c, :], sgb, MUL, t))
        nk_ok = group_norm(W[:, 3, :], SQ2, SBD, kt2)
        q_ok, q_rd = turned_q
        v_ok = natural_block(W[:, 0, :], None, [q_rd, nq_ok], between=lambda: turned_k.extend(
            turn_block(W[:, 3, :], W[:, 2, :], halves["k2"], nk_ok, nat_free2)))
        k_ok, k_rd = turned_k
        qS = W[:, 1, :].rearrange("p (c n) -> p c n", c=HB)
        kS = W[:, 2, :].rearrange("p (c n) -> p c n", c=HB)
        vS = W[:, 0, :].rearrange("p (i n) -> p i n", i=NT)
        tri, nones, negm = level[0], level[1], level[2]
        t = tt(tri, upper, ones, SUB, pe.last, ve.last)
        t = ts(negm, tri, -NEG, None, MUL, None, t)
        tri_ok = ts(nones, ones, -1.0, None, MUL, None, t)
        widths = [SEQ - P * j for j in range(NT)]
        offs = [sum(widths[:j]) for j in range(NT)]
        SPW = sum(widths)
        SP_ = T[:, 0:2 * SPW].rearrange("p (u n) -> p u n", u=2)
        A_ = T[:, 2 * SPW:4 * SPW].rearrange("p (u n) -> p u n", u=2)
        L_ = W[:, 3, :].rearrange("p (u n) -> p u n", u=4)
        w3_clear = [k_rd, nk_ok]
        sp_free, a_free, l_free = [w3_clear] * 2, [w3_clear] * 2, [w3_clear] * 4
        OUT_ = T[:, 4 * SPW:4 * SPW + BANK]
        out_free = y_ok2
        yb2, outs, held, sp_ok, a_ok = [], {}, {}, {}, {}
        li = 0

        def softplus(h, j):
            nonlocal li
            u, R, w = h % 2, slice(64 * (h % 2), 64 * (h % 2) + 64), widths[j]
            held[h, j] = b, ps, bf = bank()
            tk = mm(ps[:, 0:w], kS[R, h // 2, j * P:j * P + P], qS[R, h // 2, j * P:SEQ], True, True,
                    q_ok, k_ok, bf, signal=True, part=True)
            l = L_[:, li % 4, 0:w]
            t = act(l, ps[:, 0:w], ACT.Abs, tk, l_free[li % 4])
            t = act(l, l, ACT.Exp, t, scale=-1.0)
            t = act(l, l, ACT.Ln, t, bias=1.0)
            s_ = SP_[:, u, offs[j]:offs[j] + w]
            t = stt(s_, ps[:, 0:w], 0.0, l, MAX, ADD, t, sp_free[u])
            l_free[li % 4] = t
            li += 1
            sp_ok[h, j] = tt(s_[:, 0:P], s_[:, 0:P], upper, MUL, t)

        def weights(h, j):
            u = h % 2
            b, ps, _ = held[h, j]
            mm(ps[:, 0:P], ident, negm, False, False, sp_ok[h, j], tri_ok, part=True)
            for j2 in range(j, NT):
                tk = mm(ps[:, (j2 - j) * P:widths[j]], tri if j2 == j else nones,
                        SP_[:, u, offs[j2]:offs[j2] + widths[j2]], False, j2 == NT - 1, sp_ok[h, j2],
                        signal=j2 == NT - 1, part=True)
            a_ok[h, j] = bank_free[b] = act(A_[:, u, offs[j]:offs[j] + widths[j]], ps[:, 0:widths[j]],
                                            ACT.Exp, tk, a_free[u])
            if j == 0:
                sp_free[u] = tk

        def times_values(h):
            nonlocal out_free
            u, pair = h % 2, h // 2
            if u == 0:
                outs[pair] = bank()
            ob, ops, obf = outs[pair]
            o3 = ops.rearrange("p (i n) -> p i n", i=NT)
            for i in range(NT):
                for j in range(i + 1):
                    lo_ = offs[j] + (i - j) * P
                    tk = mm(o3[:, i, 64 * u:64 * u + 64], A_[:, u, lo_:lo_ + P],
                            vS[:, j, h * SBD:(h + 1) * SBD], j == 0, j == i, [a_ok[h, n] for n in range(NT)],
                            v_ok, obf, signal=i == NT - 1)
            a_free[u] = tk
            if u:
                outs[pair] = bank_free[ob] = act(OUT_, ops, ACT.Copy, tk, out_free)

        def pair_out(pair):
            nonlocal out_free
            b, ps, bf = bank()
            for i in range(NT):
                tk = turn(ps[:, i * P:i * P + P], OUT_[:, i * P:i * P + P], outs[pair], bf, signal=i == NT - 1)
            t = bank_free[b] = tt(OUT_, ps, ZB[:, pair, :], MUL, tk, zb_ok)
            out_free = split_act(yhi[:, 4 + pair, :], ylo[:, 4 + pair, :], OUT_, t)
            yb2.append(out_free)

        for j in reversed(range(NT)):
            softplus(0, j)
        for h in range(SBH + 1):
            for j in reversed(range(NT)):
                if h < SBH:
                    weights(h, j)
                if h + 1 < SBH:
                    softplus(h + 1, j)
                if j == NT - 2 and h:
                    times_values(h - 1)
                if j == 0 and h and h % 2 == 0:
                    pair_out((h - 1) // 2)

        fr = [pe.last, ve.last]
        g, g_ok = gates(bg2, 0, fr)
        m_ok2 = merge_first(yhi[:, 0:4, :], ylo[:, 0:4, :], HB, y_ok2, g, g_ok, fr)
        g, g_ok = gates(bg2, KD, [pe.last, m_ok2])
        parts = merge_second(yhi[:, 4:8, :], ylo[:, 4:8, :], HB, yb2, g, g_ok, fr)
        x_ok = x_in.start(sp, xw, x2_dram.rearrange("(i p) d -> p i d", p=P), fr, x2_stored)
        o_st = Arrivals(sem("s_out"))
        for b in range(2):
            def evac(c, ps, tok):
                cols = slice(b * BANK, b * BANK + BANK)
                t = tt(xw[:, c, cols], ps, xw[:, c, cols], ADD, tok, x_ok)
                end = o_st.start(sp, out[0, c * P:c * P + P, cols], xw[:, c, cols], t)
                return t
            product(False, hthi, htlo, KD, None, evac, by_k=parts)
        sp.wait((o_st.sem, o_st.count))

    block_two()
    sp.wait(x2_stored)

    with nc.Block() as block:
        @block.sync
        def _(e):
            sp.play(e)

        @block.tensor
        def _(e):
            pe.play(e)

        @block.vector
        def _(e):
            ve.play(e)

        @block.scalar
        def _(e):
            ac.play(e)

        @block.gpsimd
        def _(e):
            po.play(e)
    ctx.close()


INPUTS = ("x", "norm1_g", "w_in", "v_norm_g", "w_s", "b_s", "q_norm_g", "k_norm_g", "lambda_q1",
          "lambda_k1", "lambda_q2", "lambda_k2", "sub_norm_g", "w_up_a", "w_up_b", "w_gate", "b_gate",
          "w_out", "norm2_g", "w_rg", "b_rg", "w_re", "b_re", "w1", "w3", "w2", "norm_gain_2",
          "w_in_2", "b_gate_2", "conv_w_2", "a_log_2", "dt_bias_2", "dn_out_gain_2",
          "sb_q_gain_2", "sb_k_gain_2", "w_up_a_2", "w_up_b_2", "w_out_2")


def kernel(**inputs):
    import numpy as np
    from concourse import bacc
    from concourse.bass_utils import run_bass_kernel_spmd

    nc = bacc.Bacc("TRN2", target_bir_lowering=False, num_devices=1)
    arrays, args = {}, []
    for name in INPUTS:
        a = np.ascontiguousarray(inputs[name])
        arrays[f"in_{name}"] = a
        args.append(nc.dram_tensor(f"in_{name}", a.shape, mybir.dt.from_np(a.dtype),
                                   kind="ExternalInput").ap())
    shape = inputs["x"].shape
    args.append(nc.dram_tensor("result", shape, F32, kind="ExternalOutput").ap())
    build(nc, *args)
    r = run_bass_kernel_spmd(nc, [arrays], core_ids=[0])
    return r.results[0]["result"]
```
